# Optimizing a Trainium2 kernel written in Bass

```python
import math
import jax, jax.numpy as jnp
from jax import lax
import numpy as np

D_MODEL = 4096
BATCH = 1
SEQ = 256
DEPTH = 2

HEAD_DIM = 128
D_MIX = D_MODEL
BRANCH_WIDTH = D_MIX // 4
GLA_HEADS = BRANCH_WIDTH // HEAD_DIM
GLA_DK = HEAD_DIM // 2
GLA_DV = HEAD_DIM
GLA_RANK = 16
GLA_TAU = 16.0
GLA_CHUNK = 64
SWA_HEADS = BRANCH_WIDTH // HEAD_DIM
SWA_KV_HEADS = SWA_HEADS // 4
SWA_GROUP = SWA_HEADS // SWA_KV_HEADS
SWA_WINDOW = 128
DIFF_HEADS = BRANCH_WIDTH // HEAD_DIM
DIFF_DQK = HEAD_DIM // 2
DIFF_DV = HEAD_DIM
Q_BLOCK = 128
LRU_WIDTH = BRANCH_WIDTH
LRU_BLOCKS = BRANCH_WIDTH // HEAD_DIM
LRU_BLOCK_DIM = LRU_WIDTH // LRU_BLOCKS
LRU_C = 8.0
CONV_WIDTH = 4
NORM_EPS = 1e-6

IN_SPLITS = (
    GLA_HEADS * GLA_DK, GLA_HEADS * GLA_DK, GLA_HEADS * GLA_DV, GLA_RANK,
    SWA_HEADS * HEAD_DIM, SWA_KV_HEADS * HEAD_DIM, SWA_KV_HEADS * HEAD_DIM,
    DIFF_HEADS * 2 * DIFF_DQK, DIFF_HEADS * 2 * DIFF_DQK, DIFF_HEADS * DIFF_DV,
    LRU_WIDTH, D_MIX,
)
D_IN = sum(IN_SPLITS)

kernel_name = 'hybrid_parallel_heads_block'

def rms_norm(x, w):
    xf = x.astype(jnp.float32)
    y = xf * lax.rsqrt(jnp.mean(xf * xf, axis=-1, keepdims=True) + NORM_EPS)
    return (y * w.astype(jnp.float32)).astype(x.dtype)

def alibi_slopes(n):
    return 2.0 ** (-8.0 * jnp.arange(1, n + 1, dtype=jnp.float32) / n)

def split_cols(t, sizes):
    offs, acc = [], 0
    for s in sizes[:-1]:
        acc += s
        offs.append(acc)
    return jnp.split(t, offs, axis=-1)

def gla_mixer(q, k, v, a_lr, w_up, b_up, norm_w):
    B, S, _ = q.shape
    C, H, dk, dv = GLA_CHUNK, GLA_HEADS, GLA_DK, GLA_DV
    nc = S // C
    f32 = jnp.float32
    qf = q.astype(f32).reshape(B, nc, C, H, dk) * dk ** -0.5
    kf = k.astype(f32).reshape(B, nc, C, H, dk)
    vf = v.astype(f32).reshape(B, nc, C, H, dv)
    logit = jnp.einsum('bsr,rk->bsk', a_lr.astype(f32), w_up.astype(f32)) + b_up.astype(f32)
    g = (jax.nn.log_sigmoid(logit) / GLA_TAU).reshape(B, nc, C, H, dk)
    b = jnp.cumsum(g, axis=2)
    b_last = b[:, :, -1:]
    q_dec = qf * jnp.exp(b)
    k_dec = kf * jnp.exp(-b)
    causal = jnp.tril(jnp.ones((C, C), dtype=bool))
    A = jnp.einsum('bnihd,bnjhd->bnhij', q_dec, k_dec)
    A = jnp.where(causal, A, 0.0)
    o_intra = jnp.einsum('bnhij,bnjhv->bnihv', A, vf)
    k_state = kf * jnp.exp(b_last - b)
    U = jnp.einsum('bnjhd,bnjhv->bnhdv', k_state, vf)
    decay = jnp.exp(b_last[:, :, 0])

    def step(state, inp):
        d, u = inp
        return d[..., None] * state + u, state

    s0 = jnp.zeros((B, H, dk, dv), f32)
    _, s_start = lax.scan(step, s0, (jnp.swapaxes(decay, 0, 1), jnp.swapaxes(U, 0, 1)))
    s_start = jnp.swapaxes(s_start, 0, 1)
    o_inter = jnp.einsum('bnihd,bnhdv->bnihv', q_dec, s_start)
    o = (o_intra + o_inter).reshape(B, S, H, dv)
    o = rms_norm(o, norm_w)
    return o.reshape(B, S, H * dv).astype(v.dtype)

def with_prev_block(t, W):
    B, S, Hk, d = t.shape
    tb = t.reshape(B, S // W, W, Hk, d)
    prev = jnp.concatenate([jnp.zeros_like(tb[:, :1]), tb[:, :-1]], axis=1)
    return jnp.concatenate([prev, tb], axis=2)

def swa_mixer(q, k, v, q_norm_w, k_norm_w, sinks):
    B, S, _ = q.shape
    W = SWA_WINDOW
    nb = S // W
    q = rms_norm(q.reshape(B, S, SWA_KV_HEADS, SWA_GROUP, HEAD_DIM), q_norm_w) * HEAD_DIM ** -0.5
    k = rms_norm(k.reshape(B, S, SWA_KV_HEADS, HEAD_DIM), k_norm_w)
    v = v.reshape(B, S, SWA_KV_HEADS, HEAD_DIM)
    qb = q.reshape(B, nb, W, SWA_KV_HEADS, SWA_GROUP, HEAD_DIM)
    kb = with_prev_block(k, W)
    vb = with_prev_block(v, W)
    s = jnp.einsum('bnqhgd,bnkhd->bnhgqk', qb, kb).astype(jnp.float32)
    q_pos = jnp.arange(W)[:, None] + W
    k_pos = jnp.arange(2 * W)[None, :]
    dist = q_pos - k_pos
    blk = jnp.arange(nb)[:, None, None]
    valid = (dist >= 0) & (dist < W) & (blk * W + k_pos - W >= 0)
    slopes = alibi_slopes(SWA_HEADS).reshape(SWA_KV_HEADS, SWA_GROUP)
    s = s - slopes[:, :, None, None] * dist.astype(jnp.float32)
    s = jnp.where(valid[None, :, None, None], s, -jnp.inf)
    sink = sinks.astype(jnp.float32).reshape(1, 1, SWA_KV_HEADS, SWA_GROUP, 1, 1)
    m = jnp.maximum(jnp.max(s, axis=-1, keepdims=True), sink)
    p = jnp.exp(s - m)
    p = p / (jnp.sum(p, axis=-1, keepdims=True) + jnp.exp(sink - m))
    o = jnp.einsum('bnhgqk,bnkhd->bnqhgd', p.astype(v.dtype), vb)
    return o.reshape(B, S, SWA_HEADS * HEAD_DIM)

def diff_mixer(q, k, v, q_norm_w, k_norm_w, lq1, lk1, lq2, lk2, out_norm_w, lambda_init):
    B, S, _ = q.shape
    H = DIFF_HEADS
    q = rms_norm(q.reshape(B, S, H, 2, DIFF_DQK), q_norm_w) * DIFF_DQK ** -0.5
    k = rms_norm(k.reshape(B, S, H, 2, DIFF_DQK), k_norm_w)
    v = v.reshape(B, S, H, DIFF_DV)
    f32 = jnp.float32
    lam = (jnp.exp(jnp.sum(lq1.astype(f32) * lk1.astype(f32)))
           - jnp.exp(jnp.sum(lq2.astype(f32) * lk2.astype(f32))) + lambda_init)
    slopes = alibi_slopes(H)
    nq = S // Q_BLOCK
    qb = jnp.moveaxis(q.reshape(B, nq, Q_BLOCK, H, 2, DIFF_DQK), 1, 0)
    k_pos = jnp.arange(S)

    def block(args):
        qi, idx = args
        s = jnp.einsum('bqhcd,bkhcd->bhcqk', qi, k).astype(f32)
        q_pos = idx * Q_BLOCK + jnp.arange(Q_BLOCK)
        dist = q_pos[:, None] - k_pos[None, :]
        s = s - slopes[None, :, None, None, None] * dist.astype(f32)
        s = jnp.where(dist >= 0, s, -jnp.inf)
        p = jax.nn.softmax(s, axis=-1)
        w = p[:, :, 0] - lam * p[:, :, 1]
        return jnp.einsum('bhqk,bkhv->bqhv', w.astype(v.dtype), v)

    o = lax.map(block, (qb, jnp.arange(nq)))
    o = jnp.moveaxis(o, 0, 1).reshape(B, S, H, DIFF_DV)
    o = rms_norm(o, out_norm_w) * (1.0 - lambda_init)
    return o.reshape(B, S, H * DIFF_DV)

def rglru_mixer(x, conv_w, conv_b, w_r, b_r, w_i, b_i, lam):
    B, S, Wd = x.shape
    f32 = jnp.float32
    xc = lax.conv_general_dilated(
        x, conv_w[:, None, :].astype(x.dtype), window_strides=(1,),
        padding=[(CONV_WIDTH - 1, 0)], dimension_numbers=('NWC', 'WIO', 'NWC'),
        feature_group_count=Wd) + conv_b
    xf = xc.astype(f32)
    xh = xf.reshape(B, S, LRU_BLOCKS, LRU_BLOCK_DIM)
    r = jax.nn.sigmoid(jnp.einsum('bsni,nij->bsnj', xh, w_r.astype(f32)).reshape(B, S, Wd) + b_r.astype(f32))
    i = jax.nn.sigmoid(jnp.einsum('bsni,nij->bsnj', xh, w_i.astype(f32)).reshape(B, S, Wd) + b_i.astype(f32))
    log_a = -LRU_C * r * jax.nn.softplus(-lam.astype(f32))
    a = jnp.exp(log_a)
    u = jnp.sqrt(-jnp.expm1(2.0 * log_a)) * (i * xf)

    def combine(c1, c2):
        a1, b1 = c1
        a2, b2 = c2
        return a1 * a2, a2 * b1 + b2

    _, h = lax.associative_scan(combine, (a, u), axis=1)
    return h.astype(x.dtype)

def setup_inputs(seed: int = 0) -> dict:
    key = jax.random.key(seed)
    ks = jax.random.split(key, 24)

    def nrm(k, shape, scale):
        return jax.random.normal(k, shape, jnp.float32) * scale

    u = jax.random.uniform(ks[23], (DEPTH, LRU_WIDTH), jnp.float32, 0.9, 0.999)
    p = u ** (1.0 / LRU_C)
    return {
        'x': nrm(ks[0], (BATCH, SEQ, D_MODEL), 1.0),
        'norm_w': 1.0 + nrm(ks[1], (DEPTH, D_MODEL), 0.02),
        'w_in': nrm(ks[2], (DEPTH, D_MODEL, D_IN), D_MODEL ** -0.5),
        'w_out': nrm(ks[3], (DEPTH, D_MIX, D_MODEL), D_MIX ** -0.5),
        'gla_w_up': nrm(ks[4], (DEPTH, GLA_RANK, GLA_HEADS * GLA_DK), GLA_RANK ** -0.5),
        'gla_b_up': nrm(ks[5], (DEPTH, GLA_HEADS * GLA_DK), 0.1),
        'gla_norm_w': 1.0 + nrm(ks[6], (DEPTH, GLA_DV), 0.02),
        'swa_q_norm': 1.0 + nrm(ks[7], (DEPTH, HEAD_DIM), 0.02),
        'swa_k_norm': 1.0 + nrm(ks[8], (DEPTH, HEAD_DIM), 0.02),
        'swa_sinks': nrm(ks[9], (DEPTH, SWA_HEADS), 0.5),
        'diff_q_norm': 1.0 + nrm(ks[10], (DEPTH, DIFF_DQK), 0.02),
        'diff_k_norm': 1.0 + nrm(ks[11], (DEPTH, DIFF_DQK), 0.02),
        'diff_lq1': nrm(ks[12], (DEPTH, DIFF_DQK), 0.1),
        'diff_lk1': nrm(ks[13], (DEPTH, DIFF_DQK), 0.1),
        'diff_lq2': nrm(ks[14], (DEPTH, DIFF_DQK), 0.1),
        'diff_lk2': nrm(ks[15], (DEPTH, DIFF_DQK), 0.1),
        'diff_out_norm': 1.0 + nrm(ks[16], (DEPTH, DIFF_DV), 0.02),
        'lru_conv_w': nrm(ks[17], (DEPTH, CONV_WIDTH, LRU_WIDTH), CONV_WIDTH ** -0.5),
        'lru_conv_b': nrm(ks[18], (DEPTH, LRU_WIDTH), 0.02),
        'lru_w_r': nrm(ks[19], (DEPTH, LRU_BLOCKS, LRU_BLOCK_DIM, LRU_BLOCK_DIM), LRU_BLOCK_DIM ** -0.5),
        'lru_b_r': nrm(ks[20], (DEPTH, LRU_WIDTH), 0.02),
        'lru_w_i': nrm(ks[21], (DEPTH, LRU_BLOCKS, LRU_BLOCK_DIM, LRU_BLOCK_DIM), LRU_BLOCK_DIM ** -0.5),
        'lru_b_i': nrm(ks[22], (DEPTH, LRU_WIDTH), 0.02),
        'lru_lambda': jnp.log(p) - jnp.log1p(-p),
    }

def reference(x, norm_w, w_in, w_out, gla_w_up, gla_b_up, gla_norm_w,
              swa_q_norm, swa_k_norm, swa_sinks,
              diff_q_norm, diff_k_norm, diff_lq1, diff_lk1, diff_lq2, diff_lk2, diff_out_norm,
              lru_conv_w, lru_conv_b, lru_w_r, lru_b_r, lru_w_i, lru_b_i, lru_lambda):
    for layer in range(DEPTH):
        h = rms_norm(x, norm_w[layer])
        proj = jnp.einsum('bsd,de->bse', h, w_in[layer])
        (g_q, g_k, g_v, g_a, s_q, s_k, s_v, d_q, d_k, d_v, r_x, gate) = split_cols(proj, IN_SPLITS)
        y_gla = gla_mixer(g_q, g_k, g_v, g_a, gla_w_up[layer], gla_b_up[layer], gla_norm_w[layer])
        y_swa = swa_mixer(s_q, s_k, s_v, swa_q_norm[layer], swa_k_norm[layer], swa_sinks[layer])
        lambda_init = 0.8 - 0.6 * math.exp(-0.3 * layer)
        y_diff = diff_mixer(d_q, d_k, d_v, diff_q_norm[layer], diff_k_norm[layer],
                            diff_lq1[layer], diff_lk1[layer], diff_lq2[layer], diff_lk2[layer],
                            diff_out_norm[layer], lambda_init)
        y_lru = rglru_mixer(r_x, lru_conv_w[layer], lru_conv_b[layer], lru_w_r[layer], lru_b_r[layer],
                            lru_w_i[layer], lru_b_i[layer], lru_lambda[layer])
        y = jnp.concatenate([y_gla, y_swa, y_diff, y_lru], axis=-1)
        y = y * jax.nn.silu(gate)
        x = x + jnp.einsum('bse,ed->bsd', y, w_out[layer])
    return x


_drawn_inputs = setup_inputs


def setup_inputs(seed=0):
    import zlib

    import numpy as np

    out = dict(_drawn_inputs(seed))
    spreads = {}
    factors = {'gla_b_up': 3.14,
     'gla_norm_w': 6.559,
     'swa_q_norm': 8.0,
     'swa_k_norm': 8.0,
     'swa_sinks': 54.352,
     'diff_q_norm': 8.0,
     'diff_k_norm': 8.0,
     'diff_out_norm': 8.0,
     'lru_b_r': 48.452,
     'lru_b_i': 32.091}
    for name, (base, spread) in spreads.items():
        noise = np.random.default_rng([zlib.crc32(name.encode()), seed]).standard_normal(out[name].shape)
        drawn = base * np.exp(spread * noise) if base else spread * noise
        out[name] = __import__('jax').numpy.asarray(drawn.astype(out[name].dtype))
    for name, factor in factors.items():
        out[name] = (out[name] * factor).astype(out[name].dtype)
    return out
```

```python
import math
from contextlib import ExitStack

import concourse.bass as bass
from concourse import mybir

F32 = mybir.dt.float32
F32R = mybir.dt.float32r
ALU = mybir.AluOpType
ACT = mybir.ActivationFunctionType
AX = mybir.AxisListType

P = 128


def hybrid_trunk(nc, x, norm_w, w_in, w_out, gla_w_up, gla_b_up, gla_norm_w,
                 swa_q_norm, swa_k_norm, swa_sinks, diff_q_norm, diff_k_norm,
                 diff_lq1, diff_lk1, diff_lq2, diff_lk2, diff_out_norm,
                 lru_conv_w, lru_conv_b, lru_w_r, lru_b_r, lru_w_i, lru_b_i, lru_lambda, out):
    DEPTH, D, D_IN = w_in.shape
    SEQ = x.shape[1]
    T = SEQ // P
    KT = D // P
    NC = 512
    KG = 2
    NG = KT // KG
    RING = 4
    RANK = gla_w_up.shape[1]
    BW = D // 4
    DK = 64
    HEADS = BW // P
    GLA_QK = HEADS * DK
    EPS = 1e-6
    TAU = 16.0
    MASKED = 1e30
    assert (T, KT, NG, HEADS) == (2, 32, 16, 8)

    C_GLA = 0
    C_A = 2 * GLA_QK + BW
    C_SWA = C_A + RANK
    C_DIFF = C_SWA + BW + 2 * 2 * P
    C_RX = C_DIFF + 3 * BW
    C_GATE = C_RX + BW
    assert C_GATE + D == D_IN

    A0, B0, C0, D0, E0, O0, CHUNKS = 0, 4, 8, 16, 20, 23, 31
    N_SETUP = 14 + 5 * DEPTH
    ROUTED = 15

    Q_NORM, Q_LRU, Q_SQ, Q_SK, Q_DQ, Q_DK, Q_LAM, Q_YS, Q_SINK, Q_SLOPE, NQ = \
        0, 32, 104, 105, 106, 107, 108, 112, 144, 152, 160

    ctx = ExitStack()
    with ctx:
        def sb(name, shape, dt=F32):
            return ctx.enter_context(nc.sbuf_tensor(name, shape, dt))

        def sem(name):
            return ctx.enter_context(nc.semaphore(name))

        ahi = sb("act_hi", [P, KT, SEQ], F32R)
        alo = sb("act_lo", [P, KT, SEQ], F32R)
        F = sb("act_T", [P, KT * SEQ])
        Y = sb("mix_Y", [P, T, D])
        raw = sb("w_raw", [P, RING, KG, NC])
        whi = sb("w_hi", [P, RING, KG, NC], F32R)
        wlo = sb("w_lo", [P, RING, KG, NC], F32R)
        stage = sb("stage", [P, T, NC])
        wa_hi = sb("wa_hi", [P, KT, RANK], F32R)
        wa_lo = sb("wa_lo", [P, KT, RANK], F32R)
        ident = sb("ident", [P, P])
        tri = sb("tri", [P, P])
        suf = sb("suf", [P, P])
        chunk1 = sb("chunk1", [P, 2])
        dist = sb("dist", [P, 3 * P])
        par = sb("par", [P, DEPTH, NQ])
        pc = sb("par_now", [P, NQ])
        rstd = sb("rstd", [P, T])
        ssq = sb("ssq", [P, T, 8])
        dist_swa = sb("dist_swa", [P, 3 * P])
        small = sb("small", [P, 64])
        cst = sb("cst", [P, 4])
        one, eps, tiny = cst[:, 0:1], cst[:, 1:2], cst[:, 2:3]
        MIX = sb("mix", [P, 4352])

        gq = F[:, 0:1024].rearrange("p (t n) -> p t n", t=T)
        gk = F[:, 1024:2048].rearrange("p (t n) -> p t n", t=T)
        kT_swa = F[:, 2048:2560]
        skv = F[:, 3072:4096].rearrange("p (t n) -> p t n", t=T)
        dk = F[:, 4096:6144].rearrange("p (t n) -> p t n", t=T)
        dv = F[:, 6144:8192].rearrange("p (t n) -> p t n", t=T)

        def cut(base, size):
            return MIX[:, base:base + size]

        g_e, g_l1, g_g = cut(0, 256), cut(256, 256), cut(512, 256)
        g_eb, g_enb, g_es = cut(768, 256), cut(1024, 256), cut(1280, 256)
        g_qd, g_kd = cut(1536, 256), cut(1792, 256)
        g_ks = F[:, 4096:4608].rearrange("p (t c n) -> p t c n", t=T, c=2)
        g_q0, g_q1, g_kT = F[:, 4608:4864], F[:, 4864:5120], F[:, 5120:5376]
        g_S = F[:, 5376:5888].rearrange("p (k n) -> p k n", k=4)
        g_AT = F[:, 5888:6400]
        g_dec = F[:, 6400:6404]
        g_rs = F[:, 6404:6412]
        g_sq = cut(2048, 512)
        g_a = cut(2560, T * RANK).rearrange("p (t n) -> p t n", t=T)
        g_aT = MIX[0:RANK + 1, 2688:2944]
        g_wup = MIX[0:RANK + 1, 3072:3584]
        wa_raw = cut(3584, KT * RANK).rearrange("p (k n) -> p k n", k=KT)

        s_qn, s_qT = cut(0, 256), cut(256, 256)
        s_s, s_p, s_pT = cut(512, 384), cut(896, 384), cut(1280, 384)
        s_sm = small[:, 0:16]
        s_sq = cut(1664, 256)
        l_x = cut(1920, 260)
        l_xc = cut(2180, 256)
        l_ri = cut(2436, 512)
        l_t, l_a = F[:, 0:256], F[:, 256:512]
        l_l2, l_l1, l_u = F[:, 512:768], F[:, 768:1024], F[:, 1024:1280]
        l_h = F[:, 1280:1536]
        l_rx = F[:, 1536:1792]
        l_w = F[:, 2560:2816].rearrange("p (r n) -> p r n", r=2)
        l_par = small[:, 16:25]
        d_sq = cut(0, 512)
        d_qn, d_kn = cut(512, 256), cut(768, 256)
        d_q = (cut(1024, 256), cut(1280, 256))
        d_kT = cut(1536, 256)
        d_s = cut(1792, 768)
        d_p = cut(2560, 768)
        d_w, d_wT = cut(3328, 384), cut(3712, 384)
        d_osq = cut(4096, 256)
        d_sm = small[:, 32:64]
        x_old = cut(0, 1024).rearrange("p (t n) -> p t n", t=T)
        x_new = cut(1024, 1024).rearrange("p (t n) -> p t n", t=T)
        x_sq = cut(2048, 512)

        main = [ctx.enter_context(nc.psum_tensor(f"main{t}", [P, NC], F32)) for t in range(T)]
        M = [ctx.enter_context(nc.psum_tensor(f"mixer{k}", [P, NC], F32)) for k in range(6)]

        setup_in = sem("setup_in")
        consts = sem("consts")
        par_turned = sem("par_turned")
        par_copied = sem("par_copied")
        par_math = sem("par_math")
        par_act = sem("par_act")
        now_ready = sem("now_ready")
        w_landed = [sem(f"w_landed{s}") for s in range(RING // 2)]
        w_hi = sem("w_hi_ready")
        w_lo = sem("w_lo_ready")
        w_used = sem("w_used")
        a_hi = sem("act_hi_ready")
        a_lo = sem("act_lo_ready")
        main_ready = sem("main_ready")
        main_free = sem("main_free")
        pool_passed, pe_passed = sem("pool_passed"), sem("pe_passed")
        routed = sem("routed")
        wa_landed, wa_hi_s, wa_lo_s = sem("wa_landed"), sem("wa_hi_ready"), sem("wa_lo_ready")
        gate_mult = sem("gate_mult")
        gate_T, gate_F = sem("gate_turned"), sem("gate_copied")
        gla_zero, lru_zero, diff_zero = sem("gla_zero"), sem("lru_zero"), sem("diff_zero")
        a_sum, a_ready, a_T, a_up = sem("a_summed"), sem("a_ready"), sem("a_turned"), sem("a_up")
        G = {n: sem("gla_" + n) for n in
             "logit e l1 g sums exps dec qkd kst turned U qkT S AT ATcopied ATmasked o sq ssq ln rstd y".split()}
        S = {n: sem("swa_" + n) for n in
             "par sq ssq ln rstd qn turned qT scores s max neg p sink den rden pT pTc o y".split()}
        K = {n: sem("swak_" + n) for n in "ssq ln rstd kn turned kT".split()}
        L = {n: sem("lru_" + n) for n in
             "par rx w_landed turned x c0 c1 c2 xc gates r i t a ln2 ln1 d ix sf u h hT y".split()}
        DF = {n: sem("diff_" + n) for n in
              "par ssq sqk ln rstd qkn turned qkT scores s max neg p rp coef w0 w wT wTc o osq oln orstd y".split()}
        x_loaded, x_added, x_stored = sem("x_loaded"), sem("x_added"), sem("x_stored")
        x_squared, x_T, x_F = sem("x_squared"), sem("x_turned"), sem("x_copied")
        rs_sum, rs_ln, rs_ready = sem("rs_sum"), sem("rs_ln"), sem("rs_ready")

        block = ctx.enter_context(nc.Block())

        def ds(i, n):
            return bass.ds(i, n)

        def no_hooks(g):
            pass

        @block.sync
        def _(sp):
            def weight_chunk(n, src):
                for g in range(NG):
                    sp.wait_ge(w_lo, n * NG + (g + 1))
                    sp.dma_start(raw[:, g % RING, :, :], src(g)).then_inc(w_landed[g % RING // 2], 16)

            def from_in(layer, col):
                return lambda g: w_in[layer, g * KG * P:(g + 1) * KG * P, ds(col, NC)].rearrange(
                    "(k p) n -> p k n", p=P)

            with sp.Fori(0, DEPTH) as layer:
                n0 = layer * CHUNKS
                for first, count, col in ((0, 4, C_GLA), (4, 3, C_SWA), (7, 2, C_RX),
                                          (9, 6, C_DIFF), (15, 8, C_GATE)):
                    with sp.Fori(0, count) as i:
                        weight_chunk(n0 + i + first, from_in(layer, i * NC + col))
                with sp.Fori(0, 8) as i:
                    weight_chunk(n0 + i + O0, lambda g: w_out[
                        layer, g * KG * P:(g + 1) * KG * P, ds(i * NC, NC)].rearrange(
                            "(k p) n -> p k n", p=P))
            sp.wait_ge(x_stored, 16 * 8 * (DEPTH + 1))

        @block.gpsimd
        def _(pool):
            def after(semaphore, value):
                pool.wait_ge(semaphore, value)
                pool.sem_inc(pool_passed, 1)

            r1, r2 = MIX[:, 0:128], MIX[0:76, 128:256]
            row = 0

            def rows(dst, src):
                pool.dma_start(dst, src).then_inc(setup_in, 16)

            rows(r1[0:64, :], norm_w.rearrange("l (k p) -> (l k) p", p=P))
            rows(r1[64:128, :], lru_conv_w.rearrange("l w (n p) -> (l w n) p", p=P))
            for q, src in enumerate((lru_conv_b, lru_b_r, lru_b_i, lru_lambda)):
                rows(r2[16 * q:16 * q + 16, :], src.rearrange("l (n p) -> (l n) p", p=P))
            for q, src in enumerate((gla_norm_w, swa_q_norm, swa_k_norm, diff_out_norm)):
                rows(r2[64 + 2 * q:66 + 2 * q, :], src)
            for q, src in enumerate((diff_q_norm, diff_k_norm)):
                for c in range(2):
                    rows(r2[72 + 2 * q:74 + 2 * q, c * DK:(c + 1) * DK], src)
            for l in range(DEPTH):
                rows(par[:, l, Q_SINK:Q_SINK + HEADS], swa_sinks[l, :].partition_broadcast(P))
                for q, src in enumerate((diff_lq1, diff_lk1, diff_lq2, diff_lk2)):
                    rows(cut(512 + (4 * l + q) * DK, DK), src[l, :].partition_broadcast(P))
            pool.memset(ident[:, :], 0.0).then_inc(consts, 1)
            pool.memset(tri[:, :], 1.0 / TAU).then_inc(consts, 1)
            pool.memset(suf[:, :], 1.0 / TAU).then_inc(consts, 1)
            pool.memset(chunk1[:, :], 0.0).then_inc(consts, 1)
            pool.iota(dist[:, 0:P], pattern=[[-1, P]], base=0, channel_multiplier=1,
                      allow_small_or_imprecise_dtypes=True).then_inc(consts, 1)
            pool.iota(dist[:, P:3 * P], pattern=[[-1, 2 * P]], base=P, channel_multiplier=1,
                      allow_small_or_imprecise_dtypes=True).then_inc(consts, 1)
            pool.memset(par[:, :, Q_LAM + 1:Q_YS], 0.0)
            for h in range(HEADS):
                pool.memset(par[:, :, Q_SLOPE + h:Q_SLOPE + h + 1], -2.0 ** -(h + 1.0)).then_inc(consts, 1)
            pool.wait_ge(consts, 6 + HEADS)
            pool.affine_select(out=ident[:, :], in_=ident[:, :], compare_op=ALU.not_equal, fill=1.0,
                               base=0, pattern=[[-1, P]], channel_multiplier=1).then_inc(consts, 1)
            pool.affine_select(out=tri[:, :], in_=tri[:, :], compare_op=ALU.is_ge, fill=0.0,
                               base=0, pattern=[[1, P]], channel_multiplier=-1).then_inc(consts, 1)
            pool.affine_select(out=suf[:, :], in_=suf[:, :], compare_op=ALU.is_gt, fill=0.0,
                               base=0, pattern=[[-1, P]], channel_multiplier=1).then_inc(consts, 1)
            pool.affine_select(out=dist[:, 0:P], in_=dist[:, 0:P], compare_op=ALU.is_ge, fill=MASKED,
                               base=0, pattern=[[-1, P]], channel_multiplier=1).then_inc(consts, 1)
            pool.affine_select(out=dist[:, P:3 * P], in_=dist[:, P:3 * P], compare_op=ALU.is_ge,
                               fill=MASKED, base=P, pattern=[[-1, 2 * P]],
                               channel_multiplier=1).then_inc(consts, 1)
            pool.wait_ge(consts, 11 + HEADS)
            pool.memset(tri[0:DK, DK:P], 0.0).then_inc(consts, 1)
            pool.memset(suf[DK:P, 0:DK], 0.0).then_inc(consts, 1)
            for c in range(2):
                pool.memset(chunk1[c * DK:(c + 1) * DK, c:c + 1], 1.0 / TAU).then_inc(consts, 1)

            def load_x(f, src, i):
                after(x_added, f + 1)
                pool.dma_start(x_old, src[0, :, ds(i * NC, NC)].rearrange("(t p) n -> p t n", p=P)
                               ).then_inc(x_loaded, 16)

            def store_x(f, i):
                after(x_added, f + 2)
                pool.dma_start(out[0, :, ds(i * NC, NC)].rearrange("(t p) n -> p t n", p=P), x_new
                               ).then_inc(x_stored, 16)

            pool.sem_inc(routed, 1)
            pool.wait_ge(par_act, 2)
            with pool.Fori(0, 8) as i:
                load_x(i, x, i)
                store_x(i, i)

            def route(layer, j, dst):
                after(main_free, (layer * CHUNKS + j + 2) * T)
                pool.tensor_copy(dst, stage[:, :, :]).then_inc(routed, 1)

            def hand_rx(layer, n):
                u = layer * 8 + n
                after(routed, layer * ROUTED + n + 9)
                after(L["turned"], u + 1)
                pool.tensor_copy(l_rx.rearrange("p (t n) -> p t n", t=T),
                                 Y[:, :, ds(n * P + 3 * BW, P)]).then_inc(L["rx"], 1)

            def mask_intra(layer, i):
                u = layer * 4 + i
                AT = g_AT.rearrange("p (u i) -> p u i", u=4)
                after(G["ATcopied"], u + 1)
                pool.affine_select(out=AT, in_=AT, compare_op=ALU.is_ge, fill=0.0, base=0,
                                   pattern=[[0, 4], [1, P]], channel_multiplier=-1).then_inc(G["ATmasked"], 1)
                after(G["ATmasked"], u * 2 + 1)
                pool.memset(AT[0:DK, :, DK:P], 0.0).then_inc(G["ATmasked"], 1)

            with pool.Fori(0, DEPTH) as layer:
                after(a_lo, layer * 2 * NG + (NG + 1))
                pool.dma_start(g_wup[0:RANK, :], gla_w_up[layer, :, :]).then_inc(a_up, 16)
                pool.dma_start(g_wup[RANK:RANK + 1, :],
                               gla_b_up[ds(layer, 1), :]).then_inc(a_up, 16)
                pool.dma_start(wa_raw, w_in[layer, :, C_A:C_A + RANK].rearrange(
                    "(k p) n -> p k n", p=P)).then_inc(wa_landed, 16)
                route(layer, 0, gq)
                route(layer, 1, gk)
                with pool.Fori(0, 2) as i:
                    route(layer, i + 2, Y[:, :, ds(i * NC, NC)])
                with pool.Fori(0, 2) as i:
                    mask_intra(layer, i)
                    route(layer, i + 4, Y[:, :, ds(i * NC + BW, NC)])
                mask_intra(layer, 2)
                route(layer, 6, skv)
                mask_intra(layer, 3)
                for first, dst in ((0, lambda i: Y[:, :, ds(i * NC + 3 * BW, NC)]),
                                   (2, lambda i: Y[:, :, ds(i * NC + 2 * BW, NC)]),
                                   (4, lambda i: dk[:, :, ds(i * NC, NC)]),
                                   (6, lambda i: dv[:, :, ds(i * NC, NC)])):
                    if first == 4:
                        after(G["y"], layer * 4 + 5)
                    with pool.Fori(0, 2) as i:
                        route(layer, i + 7 + first, dst(i))
                        hand_rx(layer, i + first)
                after(DF["y"], layer * 8 + 9)
                with pool.Fori(0, 8) as i:
                    f = layer * 8 + i + 8
                    after(x_stored, layer * 128 + i * 16 + 16)
                    load_x(f, out, i)
                    store_x(f, i)

        @block.scalar
        def _(act):
            def a_split_hi(s, g, first, scale, ready, base):
                act.wait_ge(ready, base)
                for k in range(KG * g, KG * g + KG):
                    ins = act.activation(ahi[:, k, :], F[:, k * SEQ:(k + 1) * SEQ], ACT.Copy,
                                         scale=pc[:, scale + k:scale + k + 1])
                ins.then_inc(a_hi, 1)

            def chunk(n, hooks=no_hooks, before=no_hooks):
                for g in range(NG):
                    before(g)
                    if g % 2 == 0:
                        act.wait_ge(w_landed[g % RING // 2], n * (32 * (NG // RING)) + 32 * (g // RING + 1))
                        act.wait_ge(w_used, n * NG + (g + 2))
                    act.activation(whi[:, g % RING, :, :], raw[:, g % RING, :, :], ACT.Copy).then_inc(w_hi, 1)
                    hooks(g)

            def evac(n, func):
                act.wait_ge(main_ready, n + 1)
                act.activation(stage[:, 0, :], main[0][:, :], func, scale=rstd[:, 0:1]).then_inc(main_free, 1)
                act.wait_ge(w_used, n * NG + (NG + RING))
                act.activation(stage[:, 1, :], main[1][:, :], func, scale=rstd[:, 1:2]).then_inc(main_free, 1)

            def evac_raw(layer, j):
                act.wait_ge(routed, layer * ROUTED + (j + 1))
                evac(layer * CHUNKS + j, ACT.Copy)

            def evac_gate(layer, j):
                act.wait_ge(gate_F, layer * 16 + (j * 2 + 1))
                act.wait_ge(routed, layer * ROUTED + (ROUTED + 1))
                evac(layer * CHUNKS + j + ROUTED, ACT.Silu)
                act.preload_act_table_set("natural_log_exp_and_others")

            def rsqrt(dst, src, n, ln, done, u):
                act.activation(dst, src, ACT.Ln, scale=1.0 / n, bias=eps[:, :]).then_inc(ln, 1)
                act.wait_ge(ln, u)
                act.activation(dst, dst, ACT.Exp, scale=-0.5).then_inc(done, 1)

            def gla(u, g):
                if g == 3:
                    act.wait_ge(G["logit"], u + 1)
                    act.activation(g_e, M[0][:, 0:256], ACT.Abs).then_inc(G["e"], 1)
                    act.wait_ge(G["e"], u * 2 + 1)
                    act.activation(g_e, g_e, ACT.Exp, scale=-1.0).then_inc(G["e"], 1)
                    act.wait_ge(G["e"], u * 2 + 2)
                    act.activation(g_l1, g_e, ACT.Ln, bias=one[:, :]).then_inc(G["l1"], 1)
                if g == 6:
                    act.wait_ge(G["sums"], u + 1)
                    act.activation(g_eb, M[1][:, 0:256], ACT.Exp)
                    act.activation(g_enb, M[1][:, 0:256], ACT.Exp, scale=-1.0)
                    act.activation(g_es, M[1][:, 256:512], ACT.Exp).then_inc(G["exps"], 1)
                    act.activation(g_dec, M[2][:, 0:4], ACT.Exp).then_inc(G["dec"], 1)
                if g == 9:
                    act.wait_ge(G["turned"], u + 1)
                    act.activation(g_q0[0:DK, :], M[3][0:DK, 0:256], ACT.Copy)
                    act.activation(g_q1[DK:P, :], M[3][DK:P, 0:256], ACT.Copy)
                    act.activation(g_kT, M[3][:, 256:512], ACT.Copy).then_inc(G["qkT"], 1)
                if g == 11:
                    act.wait_ge(G["AT"], u + 1)
                    act.activation(g_AT, M[0][:, :], ACT.Copy).then_inc(G["ATcopied"], 1)
                if g == 14:
                    act.wait_ge(G["o"], u + 1)
                    act.activation(g_sq, M[1][:, :], ACT.Square).then_inc(G["sq"], 1)
                    act.wait_ge(G["ssq"], u + 1)
                    rsqrt(g_rs[:, 4:8], g_rs[:, 0:4], P, G["ln"], G["rstd"], u + 1)

            def swa(u, g):
                if g == 1:
                    act.wait_ge(S["ssq"], u + 1)
                    rsqrt(s_sm[:, 2:4], s_sm[:, 0:2], P, S["ln"], S["rstd"], u + 1)
                if g == 7:
                    act.wait_ge(S["turned"], u + 1)
                    act.activation(s_qT, M[0][:, 0:256], ACT.Copy, scale=pc[:, Q_SQ:Q_SQ + 1]).then_inc(S["qT"], 1)
                if g == 10:
                    act.wait_ge(S["neg"], u + 1)
                    act.activation(s_p[:, 0:P], s_s[:, 0:P], ACT.Exp, bias=s_sm[:, 6:7],
                                   accum_out=s_sm[:, 8:9])
                    act.activation(s_p[:, P:3 * P], s_s[:, P:3 * P], ACT.Exp, bias=s_sm[:, 7:8],
                                   accum_out=s_sm[:, 9:10]).then_inc(S["p"], 1)
                    act.activation(s_sm[:, 10:12], s_sm[:, 6:8], ACT.Exp, bias=s_sm[:, 14:15]).then_inc(S["sink"], 1)
                
            def lru(layer, u, i, g):
                if g == 0:
                    act.wait_ge(L["gates"], u + 1)
                    act.dma_start(l_w[:, 0, :], lru_w_r[layer, ds(i, 1), :, :].rearrange(
                        "b i j -> i (b j)")).then_inc(L["w_landed"], 16)
                    act.dma_start(l_w[:, 1, :], lru_w_i[layer, ds(i, 1), :, :].rearrange(
                        "b i j -> i (b j)")).then_inc(L["w_landed"], 16)
                if g == 10:
                    act.wait_ge(L["gates"], u + 2)
                    act.activation(l_ri[:, 0:256], M[5][:, 0:256], ACT.Sigmoid, bias=l_par[:, 5:6]).then_inc(L["r"], 1)
                    act.activation(l_ri[:, 256:512], M[5][:, 256:512], ACT.Sigmoid,
                                   bias=l_par[:, 6:7]).then_inc(L["i"], 1)
                if g == 11:
                    act.wait_ge(L["r"], u + 1)
                    act.activation(l_t, l_ri[:, 0:256], ACT.Tanh, scale=l_par[:, 7:8],
                                   bias=tiny[:, :]).then_inc(L["t"], 1)
                    act.preload_act_table_set("natural_log_exp_and_others")
                    act.activation(l_a, l_ri[:, 0:256], ACT.Exp, scale=l_par[:, 8:9]).then_inc(L["a"], 1)
                if g == 12:
                    act.wait_ge(L["t"], u + 1)
                    act.activation(l_l2, l_t, ACT.Ln, scale=2.0)
                    act.activation(l_l1, l_t, ACT.Ln, bias=one[:, :]).then_inc(L["ln1"], 1)
                if g == 13:
                    act.wait_ge(L["d"], u + 1)
                    act.activation(l_l2, l_l2, ACT.Exp, scale=0.5).then_inc(L["sf"], 1)

            def diff(u, col, s):
                if s == 0:
                    act.wait_ge(DF["ssq"], u + 1)
                    rsqrt(d_sm[:, 8:16], d_sm[:, 0:8], DK, DF["ln"], DF["rstd"], u + 1)
                if s == 2:
                    act.wait_ge(DF["turned"], u + 1)
                    act.activation(d_q[0][0:DK, :], M[0][0:DK, 0:256], ACT.Copy, scale=pc[0:DK, Q_DQ:Q_DQ + 1])
                    act.activation(d_q[1][DK:P, :], M[0][DK:P, 0:256], ACT.Copy, scale=pc[DK:P, Q_DQ:Q_DQ + 1])
                    act.activation(d_kT, M[0][:, 256:512], ACT.Copy, scale=pc[:, Q_DK:Q_DK + 1]).then_inc(DF["qkT"], 1)
                if s == 4:
                    act.wait_ge(DF["neg"], u + 1)
                    for c in range(2):
                        b = c * 384
                        act.activation(d_p[:, b:b + P], d_s[:, b:b + P], ACT.Exp,
                                       bias=d_sm[:, 20 + c:21 + c], accum_out=d_sm[:, 24 + c:25 + c])
                        ins = act.activation(d_p[:, b + P:b + 384], d_s[:, b + P:b + 384], ACT.Exp,
                                             bias=d_sm[:, 22 + c:23 + c], accum_out=d_sm[:, 26 + c:27 + c])
                    ins.then_inc(DF["p"], 1)
                if s == 6:
                    act.wait_ge(DF["wT"], u + 1)
                    act.activation(d_wT, M[3][:, 0:384], ACT.Copy).then_inc(DF["wTc"], 1)
                if s == 7:
                    act.wait_ge(DF["o"], u + 1)
                    for t in range(T):
                        ins = act.activation(d_osq[:, t * P:(t + 1) * P], M[4][:, t * P:(t + 1) * P], ACT.Square,
                                             accum_out=small[:, 26 + t:27 + t])
                    ins.then_inc(DF["osq"], 1)
                    act.wait_ge(DF["osq"], u + 1)
                    rsqrt(small[:, 28:30], small[:, 26:28], P, DF["oln"], DF["orstd"], u + 1)
                    act.wait_ge(DF["orstd"], u + 1)
                    for t in range(T):
                        ins = act.activation(Y[:, t, ds(col, P)], M[4][:, t * P:(t + 1) * P], ACT.Copy,
                                             scale=small[:, 28 + t:29 + t])
                    ins.then_inc(DF["y"], 1)

            def gate_out(layer, j, g, hooks=(8, 11)):
                if g in hooks:
                    half = hooks.index(g)
                    act.wait_ge(gate_T, layer * 16 + (j * 2 + half + 1))
                    act.activation(F[:, ds(j * 1024 + half * 512, 512)], M[5][:, :], ACT.Copy).then_inc(gate_F, 1)

            def square_x(f, i):
                act.wait_ge(x_added, f + 2)
                for t in range(T):
                    act.wait_ge(x_squared, f * T + (t + 1))
                    act.activation(x_sq, x_new[:, t, :], ACT.Square,
                                   accum_out=ssq[:, t, ds(i, 1)]).then_inc(x_squared, 1)

            def copy_x(f, i, half):
                act.wait_ge(x_T, f * 2 + half + 1)
                act.activation(F[:, ds(i * 1024 + half * 512, 512)], M[half][:, :], ACT.Copy).then_inc(x_F, 1)

            def finish_x(f, i):
                square_x(f, i)
                for half in range(2):
                    copy_x(f, i, half)

            act.preload_act_table_set("natural_log_exp_and_others")
            act.sem_inc(main_free, T)
            act.sem_inc(gate_F, 1)
            act.sem_inc(x_squared, 1)
            act.sem_inc(DF["y"], 1)
            act.wait_ge(par_math, 5)
            act.activation(small[:, 0:4], small[:, 0:4], ACT.Exp).then_inc(par_act, 1)
            act.wait_ge(par_math, 6)
            act.activation(cut(1600, 16), cut(1600, 16), ACT.Exp, scale=-1.0).then_inc(par_act, 1)
            with act.Fori(0, 8) as i:
                finish_x(i, i)

            with act.Fori(0, DEPTH) as layer:
                n0 = layer * CHUNKS
                act.wait_ge(rs_sum, layer + 1)
                rsqrt(rstd[:, :], small[:, 30:32], D, rs_ln, rs_ready, layer + 1)
                act.wait_ge(now_ready, layer + 1)

                act.wait_ge(w_used, n0 * NG + RING)

                def split_x(g):
                    a_split_hi(layer * 2, g, 0, Q_NORM, x_F, layer * 16 + (g + 3))

                def split_y(g):
                    if g == 0:
                        act.wait_ge(w_used, n0 * NG + O0 * NG + RING)
                    a_split_hi(layer * 2 + 1, g, 0, Q_YS, gate_F, layer * 16 + (g + 2))

                chunk(n0, before=split_x)
                with act.Fori(0, 3) as i:
                    chunk(n0 + i + 1, lambda g: evac_raw(layer, i) if g == 1 else None)
                act.wait_ge(x_stored, layer * 128 + 128)
                act.wait_ge(wa_landed, layer * 16 + 16)
                act.activation(wa_hi[:, :, :], wa_raw, ACT.Copy).then_inc(wa_hi_s, 1)
                act.wait_ge(a_sum, layer + 1)
                for t in range(T):
                    ins = act.activation(g_a[:, t, :], M[0][:, t * RANK:(t + 1) * RANK], ACT.Copy,
                                         scale=rstd[:, t:t + 1])
                ins.then_inc(a_ready, 1)
                act.wait_ge(gla_zero, layer + 1)
                act.wait_ge(a_T, layer + 1)
                act.activation(g_aT[0:RANK, :], M[1][0:RANK, 0:256], ACT.Copy).then_inc(a_ready, 1)
                with act.Fori(0, 4) as i:

                    def hooks_b(g):
                        if g == 1:
                            evac_raw(layer, i + 3)
                        gla(layer * 4 + i, g)
                    chunk(n0 + i + B0, hooks_b)
                act.wait_ge(K["ssq"], layer + 1)
                rsqrt(s_sm[:, 4:8], s_sm[:, 0:4], P, K["ln"], K["rstd"], layer + 1)
                act.wait_ge(K["turned"], layer + 1)
                act.activation(kT_swa, M[0][:, :], ACT.Copy, scale=pc[:, Q_SK:Q_SK + 1]).then_inc(K["kT"], 1)
                with act.Fori(0, 8) as i:
                    u = layer * 8 + i

                    def hooks_c(g):
                        if g == 1:
                            evac_raw(layer, i + 7)
                        swa(u, g)
                        lru(layer, u, i, g)
                    chunk(n0 + i + C0, hooks_c)
                with act.Fori(0, 4) as i:

                    def hooks_d(g):
                        if g == 1:
                            evac_gate(layer, i)
                        for h in range(2):
                            s = g - 8 * h
                            if 0 <= s < 8:
                                diff(layer * 8 + i * 2 + h, i * 2 * P + (h * P + 2 * BW), s)
                        gate_out(layer, i, g)
                    chunk(n0 + i + D0, hooks_d)
                with act.Fori(0, 3) as i:

                    def hooks_e(g):
                        if g == 1:
                            evac_gate(layer, i + 4)
                        gate_out(layer, i + 4, g)
                    chunk(n0 + i + E0, hooks_e)

                def hooks_o(g):
                    if g == 1:
                        evac_gate(layer, 7)
                    gate_out(layer, 7, g)
                chunk(n0 + O0, hooks_o, before=split_y)
                with act.Fori(0, 7) as i:

                    def hooks_x(g):
                        f = layer * 8 + i + 8
                        if g == 4:
                            square_x(f, i)
                        if g in (9, 10):
                            copy_x(f, i, g - 9)
                    chunk(n0 + i + (O0 + 1), hooks_x)
                finish_x(layer * 8 + 15, 7)

        @block.vector
        def _(dve):
            def a_split_lo(s, g, scale):
                dve.wait_ge(a_hi, s * NG + (g + 1))
                for k in range(KG * g, KG * g + KG):
                    ins = dve.scalar_tensor_tensor(
                        out=alo[:, k, :], in0=F[:, k * SEQ:(k + 1) * SEQ], scalar=pc[:, scale + k:scale + k + 1],
                        in1=ahi[:, k, :].bitcast(F32), op0=ALU.mult, op1=ALU.subtract)
                ins.then_inc(a_lo, 1)

            def chunk(n, hooks=no_hooks, before=no_hooks):
                for g in range(NG):
                    before(g)
                    dve.wait_ge(w_hi, n * NG + (g + 1))
                    dve.tensor_tensor(wlo[:, g % RING, :, :], raw[:, g % RING, :, :],
                                      whi[:, g % RING, :, :].bitcast(F32), ALU.subtract).then_inc(w_lo, 1)
                    hooks(g)

            def gla(layer, u, i, g):
                vcol = i * 2 * P
                if g == 3:
                    dve.wait_ge(G["l1"], u + 1)
                    dve.scalar_tensor_tensor(out=g_g, in0=M[0][:, 0:256], scalar=0.0, in1=g_l1,
                                             op0=ALU.min, op1=ALU.subtract).then_inc(G["g"], 1)
                if g == 6:
                    dve.wait_ge(G["exps"], u + 1)
                    dve.wait_ge(routed, layer * ROUTED + 5)
                    q = gq[:, :, ds(i * P, P)]
                    k = gk[:, :, ds(i * P, P)]
                    v3 = lambda a: a.rearrange("p (t n) -> p t n", t=T)
                    dve.scalar_tensor_tensor(out=v3(g_qd), in0=q, scalar=DK ** -0.5, in1=v3(g_eb),
                                             op0=ALU.mult, op1=ALU.mult)
                    dve.tensor_tensor(v3(g_kd), k, v3(g_enb), ALU.mult).then_inc(G["qkd"], 1)
                    for c in range(2):
                        r = slice(c * DK, (c + 1) * DK)
                        ins = dve.tensor_tensor(g_ks[r, :, c, :], gk[r, :, ds(i * P, P)],
                                                v3(g_es)[r, :, :], ALU.mult)
                    ins.then_inc(G["kst"], 1)
                if g == 9:
                    dve.wait_ge(G["U"], u + 1)
                    dve.wait_ge(G["dec"], u + 1)
                    for c, (bank, off) in enumerate(((4, 0), (4, 256), (5, 0))):
                        if c:
                            dve.wait_ge(G["S"], u * 3 + c)
                        for h in range(2):
                            r = slice(h * DK, (h + 1) * DK)
                            src = M[bank][r, off + h * P:off + (h + 1) * P]
                            if c == 0:
                                ins = dve.tensor_copy(g_S[r, 1, :], src)
                            else:
                                ins = dve.scalar_tensor_tensor(out=g_S[r, c + 1, :], in0=g_S[r, c, :],
                                                               scalar=g_dec[r, c:c + 1], in1=src,
                                                               op0=ALU.mult, op1=ALU.add)
                        ins.then_inc(G["S"], 1)
                if g == 14:
                    dve.wait_ge(G["sq"], u + 1)
                    dve.tensor_reduce(g_rs[:, 0:4], g_sq.rearrange("p (k n) -> p k n", k=4), AX.X,
                                      ALU.add).then_inc(G["ssq"], 1)
                    dve.wait_ge(G["rstd"], u + 1)
                    for t in range(T):
                        for h in range(2):
                            b = (2 * t + h)
                            ins = dve.tensor_scalar(Y[:, t, ds(vcol + h * P, P)], M[1][:, b * P:(b + 1) * P],
                                                    g_rs[:, 4 + b:5 + b], None, ALU.mult)
                    ins.then_inc(G["y"], 1)

            def swa(u, i, g):
                if g == 0:
                    dve.tensor_copy(s_sm[:, 14:16].unsqueeze(2), pc[:, Q_SINK:Q_SINK + 16].rearrange(
                        "p (q h) -> p q h", q=2)[:, :, ds(i, 1)]).then_inc(S["par"], 1)
                    q = Y[:, :, ds(i * P + BW, P)]
                    sq = s_sq.rearrange("p (t n) -> p t n", t=T)
                    dve.tensor_tensor(sq, q, q, ALU.mult).then_inc(S["sq"], 1)
                    dve.wait_ge(S["sq"], u + 1)
                    dve.tensor_reduce(s_sm[:, 0:2], sq, AX.X, ALU.add).then_inc(S["ssq"], 1)
                if g == 1:
                    dve.wait_ge(S["rstd"], u + 1)
                    for t in range(T):
                        ins = dve.tensor_scalar(s_qn[:, t * P:(t + 1) * P], Y[:, t, ds(i * P + BW, P)],
                                                s_sm[:, 2 + t:3 + t], None, ALU.mult)
                    ins.then_inc(S["qn"], 1)
                if g == 9:
                    dve.wait_ge(S["scores"], u + 1)
                    dve.wait_ge(S["par"], u + 1)
                    dve.scalar_tensor_tensor(out=s_s, in0=dist_swa[:, :], scalar=s_sm[:, 15:16],
                                             in1=M[1][:, 0:384], op0=ALU.mult, op1=ALU.add).then_inc(S["s"], 1)
                    dve.wait_ge(S["s"], u + 1)
                    dve.tensor_reduce(s_sm[:, 4:5], s_s[:, 0:P], AX.X, ALU.max)
                    dve.tensor_reduce(s_sm[:, 5:6], s_s[:, P:3 * P], AX.X, ALU.max).then_inc(S["max"], 1)
                    dve.wait_ge(S["max"], u + 1)
                    dve.tensor_scalar(s_sm[:, 6:8], s_sm[:, 4:6], s_sm[:, 14:15], -1.0, ALU.max,
                                      ALU.mult).then_inc(S["neg"], 1)
                if g == 11:
                    dve.wait_ge(S["sink"], u + 1)
                    dve.tensor_tensor(s_sm[:, 12:14], s_sm[:, 8:10], s_sm[:, 10:12], ALU.add).then_inc(S["den"], 1)
                    dve.wait_ge(S["den"], u + 1)
                    dve.reciprocal(s_sm[:, 12:14], s_sm[:, 12:14]).then_inc(S["rden"], 1)
                if g == 12:
                    dve.wait_ge(S["pT"], u + 1)
                    dve.tensor_copy(s_pT, M[2][:, 0:384]).then_inc(S["pTc"], 1)
                if g == 14:
                    dve.wait_ge(S["o"], u + 1)
                    dve.wait_ge(S["rden"], u + 1)
                    for t in range(T):
                        ins = dve.tensor_scalar(Y[:, t, ds(i * P + BW, P)], M[3][:, t * P:(t + 1) * P],
                                                s_sm[:, 12 + t:13 + t], None, ALU.mult)
                    ins.then_inc(S["y"], 1)

            def lru(u, i, g):
                if g == 0:
                    dve.tensor_copy(l_par.unsqueeze(2), pc[:, Q_LRU:Q_LRU + 72].rearrange("p (q n) -> p q n", q=9)[:, :, ds(i, 1)]
                                    ).then_inc(L["par"], 1)
                if g == 7:
                    dve.wait_ge(L["turned"], u + 2)
                    dve.tensor_copy(l_x[:, 3:3 + SEQ], M[4][:, 0:256]).then_inc(L["x"], 1)
                    dve.wait_ge(L["x"], u + 1)
                    dve.wait_ge(L["par"], u + 1)
                    dve.tensor_scalar(l_xc, l_x[:, 3:3 + SEQ], l_par[:, 3:4], l_par[:, 4:5], ALU.mult,
                                      ALU.add).then_inc(L["c0"], 1)
                    for j, (prev, done) in enumerate((("c0", "c1"), ("c1", "c2"), ("c2", "xc"))):
                        dve.wait_ge(L[prev], u + 1)
                        dve.scalar_tensor_tensor(out=l_xc, in0=l_x[:, j:j + SEQ], scalar=l_par[:, j:j + 1],
                                                 in1=l_xc, op0=ALU.mult, op1=ALU.add).then_inc(L[done], 1)
                if g == 12:
                    dve.wait_ge(L["i"], u + 1)
                    dve.tensor_tensor(l_u, l_ri[:, 256:512], l_xc, ALU.mult).then_inc(L["ix"], 1)
                    dve.wait_ge(L["ln1"], u + 1)
                    dve.tensor_tensor(l_l2, l_l2, l_l1, ALU.subtract).then_inc(L["d"], 1)
                if g == 13:
                    dve.wait_ge(L["sf"], u + 1)
                    dve.wait_ge(L["ix"], u + 1)
                    dve.tensor_tensor(l_u, l_u, l_l2, ALU.mult).then_inc(L["u"], 1)
                    dve.wait_ge(L["u"], u + 1)
                    dve.wait_ge(L["a"], u + 1)
                    dve.tensor_tensor_scan(l_h, l_a, l_u, 0.0, ALU.mult, ALU.add).then_inc(L["h"], 1)
                if g == 15:
                    dve.wait_ge(L["hT"], u + 1)
                    dve.tensor_copy(Y[:, :, ds(i * P + 3 * BW, P)],
                                    M[4][:, 256:512].rearrange("p (t n) -> p t n", t=T)).then_inc(L["y"], 1)

            def diff(u, head, s):
                hcol = head * P
                v3 = lambda a: a.rearrange("p (t n) -> p t n", t=T)
                q, k = Y[:, :, ds(hcol + 2 * BW, P)], dk[:, :, ds(hcol, P)]
                if s == 0:
                    dve.tensor_copy(d_sm[:, 28:29], pc[:, ds(head + Q_SLOPE, 1)]).then_inc(DF["par"], 1)
                    dve.tensor_tensor(v3(d_sq[:, 0:256]), q, q, ALU.mult)
                    dve.tensor_tensor(v3(d_sq[:, 256:512]), k, k, ALU.mult).then_inc(DF["sqk"], 1)
                    dve.wait_ge(DF["sqk"], u + 1)
                    dve.tensor_reduce(d_sm[:, 0:8], d_sq.rearrange("p (k n) -> p k n", k=8), AX.X,
                                      ALU.add).then_inc(DF["ssq"], 1)
                    dve.wait_ge(DF["rstd"], u + 1)
                    for src, dst, b in ((q, d_qn, 8), (k, d_kn, 12)):
                        for t in range(T):
                            ins = dve.tensor_tensor(
                                dst[:, t * P:(t + 1) * P].rearrange("p (c n) -> p c n", c=2),
                                src[:, t, :].rearrange("p (c n) -> p c n", c=2),
                                d_sm[:, b + 2 * t:b + 2 * t + 2].unsqueeze(2).to_broadcast([P, 2, DK]), ALU.mult)
                    ins.then_inc(DF["qkn"], 1)
                if s == 3:
                    dve.wait_ge(DF["scores"], u + 1)
                    for c in range(2):
                        ins = dve.scalar_tensor_tensor(out=d_s[:, c * 384:(c + 1) * 384], in0=dist[:, :],
                                                       scalar=d_sm[:, 28:29], in1=M[1 + c][:, 0:384],
                                                       op0=ALU.mult, op1=ALU.add)
                    ins.then_inc(DF["s"], 1)
                    dve.wait_ge(DF["s"], u + 1)
                    s2 = d_s.rearrange("p (c n) -> p c n", c=2)
                    dve.tensor_reduce(d_sm[:, 16:18], s2[:, :, 0:P], AX.X, ALU.max)
                    dve.tensor_reduce(d_sm[:, 18:20], s2[:, :, P:384], AX.X, ALU.max).then_inc(DF["max"], 1)
                    dve.wait_ge(DF["max"], u + 1)
                    dve.tensor_scalar(d_sm[:, 20:24], d_sm[:, 16:20], -1.0, None, ALU.mult).then_inc(DF["neg"], 1)
                if s == 5:
                    dve.wait_ge(DF["p"], u + 1)
                    dve.reciprocal(d_sm[:, 24:28], d_sm[:, 24:28]).then_inc(DF["rp"], 1)
                    dve.wait_ge(DF["rp"], u + 1)
                    for t in range(T):
                        ins = dve.tensor_scalar(d_sm[:, 25 + 2 * t:26 + 2 * t], d_sm[:, 25 + 2 * t:26 + 2 * t],
                                                pc[:, Q_LAM:Q_LAM + 1], None, ALU.mult)
                    ins.then_inc(DF["coef"], 1)
                    dve.tensor_scalar(d_w[:, 0:P], d_p[:, 0:P], d_sm[:, 24:25], None, ALU.mult)
                    dve.tensor_scalar(d_w[:, P:384], d_p[:, P:384], d_sm[:, 26:27], None,
                                      ALU.mult).then_inc(DF["w0"], 1)
                    dve.wait_ge(DF["coef"], u + 1)
                    dve.wait_ge(DF["w0"], u + 1)
                    dve.scalar_tensor_tensor(out=d_w[:, 0:P], in0=d_p[:, 384:512], scalar=d_sm[:, 25:26],
                                             in1=d_w[:, 0:P], op0=ALU.mult, op1=ALU.add)
                    dve.scalar_tensor_tensor(out=d_w[:, P:384], in0=d_p[:, 512:768], scalar=d_sm[:, 27:28],
                                             in1=d_w[:, P:384], op0=ALU.mult, op1=ALU.add).then_inc(DF["w"], 1)

            def gate_mult_y(layer, j):
                dve.wait_ge(main_free, (layer * CHUNKS + j + ROUTED + 2) * T)
                dve.tensor_tensor(stage[:, :, :], stage[:, :, :], Y[:, :, ds(j * NC, NC)],
                                  ALU.mult).then_inc(gate_mult, 1)

            def add_x(layer, i):
                f = layer * 8 + i + 8
                dve.wait_ge(x_loaded, f * 16 + 16)
                dve.wait_ge(x_stored, f * 16)
                dve.wait_ge(x_F, f * 2 + 2)
                n = layer * CHUNKS + i + O0
                dve.wait_ge(main_ready, n + 1)
                dve.tensor_tensor(x_new[:, 0, :], x_old[:, 0, :], main[0][:, :], ALU.add).then_inc(main_free, 1)
                dve.wait_ge(w_used, n * NG + (NG + RING))
                dve.tensor_tensor(x_new[:, 1, :], x_old[:, 1, :], main[1][:, :], ALU.add).then_inc(main_free, 1)
                dve.wait_ge(main_free, (n + 2) * T)
                dve.sem_inc(x_added, 1)

            def x_rms(layer1):
                dve.wait_ge(x_squared, layer1 * 16 + 1)
                dve.tensor_reduce(small[:, 30:32], ssq[:, :, :], AX.X, ALU.add).then_inc(rs_sum, 1)


            dve.sem_inc(w_lo, RING)
            dve.sem_inc(a_lo, 1)
            dve.sem_inc(x_added, 1)
            dve.memset(one, 1.0).then_inc(par_math, 1)
            dve.memset(eps, EPS).then_inc(par_math, 1)
            dve.memset(tiny, 1e-19).then_inc(par_math, 1)
            dve.wait_ge(setup_in, N_SETUP * 16)
            lq = cut(512, 512).rearrange("p (l q n) -> p l q n", l=2, q=4)
            for l in range(DEPTH):
                for s in range(2):
                    k = 2 * l + s
                    ins = dve.tensor_tensor_reduce(cut(1024 + k * DK, DK), lq[:, l, 2 * s, :],
                                                   lq[:, l, 2 * s + 1, :], 1.0, 0.0, ALU.mult, ALU.add,
                                                   small[:, k:k + 1])
            ins.then_inc(par_math, 1)
            dve.wait_ge(par_turned, 1)
            norm = par[:, :, Q_NORM:Q_NORM + KT]
            dve.tensor_copy(norm, M[0][:, 0:64].rearrange("p (l k) -> p l k", l=2)).then_inc(par_copied, 1)
            dve.tensor_copy(par[:, :, Q_LRU:Q_LRU + 32],
                            M[0][:, 64:128].rearrange("p (l k) -> p l k", l=2)).then_inc(par_copied, 1)
            m1 = M[1]
            for q in range(4):
                dve.tensor_copy(par[:, :, Q_LRU + 32 + 8 * q:Q_LRU + 40 + 8 * q],
                                m1[:, 16 * q:16 * q + 16].rearrange("p (l k) -> p l k", l=2)).then_inc(par_copied, 1)
            for col, off, scale in ((Q_SQ, 66, P ** -0.5), (Q_SK, 68, 1.0), (Q_DQ, 72, DK ** -0.5), (Q_DK, 74, 1.0)):
                for l in range(DEPTH):
                    dve.tensor_scalar(par[:, l, col:col + 1], m1[:, off + l:off + l + 1], scale, None,
                                      ALU.mult).then_inc(par_copied, 1)
            ys = par[:, :, Q_YS:Q_YS + KT]
            dve.memset(ys, 1.0).then_inc(par_math, 1)
            dve.wait_ge(par_math, 5)
            for l in range(DEPTH):
                lam_init = 0.8 - 0.6 * math.exp(-0.3 * l)
                dve.tensor_scalar(ys[:, l, 0:8], ys[:, l, 0:8], m1[:, 64 + l:65 + l], None,
                                  ALU.mult).then_inc(par_copied, 1)
                dve.tensor_scalar(ys[:, l, 16:24], ys[:, l, 16:24], m1[:, 70 + l:71 + l], 1.0 - lam_init,
                                  ALU.mult, ALU.mult).then_inc(par_copied, 1)
            dve.wait_ge(par_copied, 18)
            lam = cut(1584, 16)
            dve.tensor_copy(lam.rearrange("p (l n) -> p l n", l=2), par[:, :, Q_LRU + 56:Q_LRU + 64]
                            ).then_inc(par_copied, 1)
            dve.wait_ge(par_copied, 19)
            dve.tensor_scalar(cut(1600, 16), lam, -1.0, None, ALU.mult).then_inc(par_copied, 1)
            dve.wait_ge(par_copied, 20)
            dve.tensor_tensor(cut(1600, 16), cut(1600, 16), lam, ALU.max).then_inc(par_math, 1)
            dve.wait_ge(par_act, 2)
            chain = [20]

            def link(ins):
                chain[0] += 1
                ins.then_inc(par_copied, 1)
                dve.wait_ge(par_copied, chain[0])

            e, s, s2, a = cut(1600, 16), cut(1616, 16), cut(1632, 16), cut(1648, 16)
            link(dve.tensor_scalar(s2, e, 2.0, None, ALU.add))
            link(dve.reciprocal(s2, s2))
            link(dve.tensor_tensor(s, e, s2, ALU.mult))
            link(dve.tensor_tensor(s2, s, s, ALU.mult))
            link(dve.tensor_scalar(a, s2, 1.0 / 15, None, ALU.mult))
            for n in (13, 11, 9, 7, 5, 3):
                link(dve.scalar_tensor_tensor(out=a, in0=a, scalar=1.0 / n, in1=s2, op0=ALU.add, op1=ALU.mult))
            link(dve.scalar_tensor_tensor(out=a, in0=a, scalar=1.0, in1=s, op0=ALU.add, op1=ALU.mult))
            link(dve.tensor_scalar(a, a, 2.0, None, ALU.mult))
            link(dve.tensor_scalar(lam, lam, -1.0, 0.0, ALU.mult, ALU.max))
            link(dve.tensor_tensor(a, a, lam, ALU.add))
            a2 = a.rearrange("p (l n) -> p l n", l=2)
            link(dve.tensor_scalar(par[:, :, Q_LRU + 56:Q_LRU + 64], a2, 8.0, None, ALU.mult))
            link(dve.tensor_scalar(par[:, :, Q_LRU + 64:Q_LRU + 72], a2, -8.0, None, ALU.mult))
            for l in range(DEPTH):
                lam_init = 0.8 - 0.6 * math.exp(-0.3 * l)
                link(dve.tensor_scalar(small[:, 2 * l:2 * l + 1], small[:, 2 * l:2 * l + 1], lam_init, None, ALU.add))
                link(dve.tensor_tensor(par[:, l, Q_LAM:Q_LAM + 1], small[:, 2 * l + 1:2 * l + 2],
                                       small[:, 2 * l:2 * l + 1], ALU.subtract))
            dve.wait_ge(consts, 15 + HEADS)
            link(dve.tensor_scalar(dist_swa[:, :], dist[:, :], float(P), MASKED, ALU.is_ge, ALU.mult))
            link(dve.tensor_tensor(dist_swa[:, :], dist_swa[:, :], dist[:, :], ALU.max))

            dve.wait_ge(x_loaded, 16)
            dve.tensor_copy(x_new, x_old).then_inc(x_added, 1)
            with dve.Fori(1, 8) as i:
                dve.wait_ge(x_loaded, i * 16 + 16)
                dve.wait_ge(x_F, i * 2 + 2)
                dve.wait_ge(x_stored, i * 16)
                dve.tensor_copy(x_new, x_old).then_inc(x_added, 1)

            with dve.Fori(0, DEPTH) as layer:
                n0 = layer * CHUNKS
                dve.wait_ge(a_lo, layer * 2 * NG + 1)
                dve.tensor_copy(pc[:, :], par[:, ds(layer, 1), :].rearrange("p a n -> p (a n)")
                                ).then_inc(now_ready, 1)
                x_rms(layer + 1)
                dve.wait_ge(now_ready, layer + 1)
                dve.wait_ge(w_used, n0 * NG + RING)
                chunk(n0, before=lambda g: a_split_lo(layer * 2, g, Q_NORM))
                with dve.Fori(0, 3) as i:
                    chunk(n0 + i + 1)
                dve.wait_ge(wa_hi_s, layer + 1)
                dve.tensor_tensor(wa_lo[:, :, :], wa_raw, wa_hi[:, :, :].bitcast(F32),
                                  ALU.subtract).then_inc(wa_lo_s, 1)
                dve.memset(g_ks, 0.0)
                dve.memset(g_q0, 0.0)
                dve.memset(g_q1, 0.0)
                dve.memset(g_S[:, 0, :], 0.0)
                dve.memset(g_aT, 1.0).then_inc(gla_zero, 1)
                with dve.Fori(0, 4) as i:
                    chunk(n0 + i + B0, lambda g: gla(layer, layer * 4 + i, i, g))
                dve.wait_ge(routed, layer * ROUTED + 8)
                for t in range(T):
                    for h in range(2):
                        b = 2 * h + t
                        k = skv[:, t, h * P:(h + 1) * P]
                        ins = dve.tensor_tensor_reduce(cut(b * P, P), k, k, 1.0, 0.0, ALU.mult, ALU.add,
                                                       s_sm[:, b:b + 1])
                ins.then_inc(K["ssq"], 1)
                dve.wait_ge(K["rstd"], layer + 1)
                for t in range(T):
                    for h in range(2):
                        b = 2 * h + t
                        ins = dve.tensor_scalar(cut(b * P, P), skv[:, t, h * P:(h + 1) * P],
                                                s_sm[:, 4 + b:5 + b], None, ALU.mult)
                ins.then_inc(K["kn"], 1)
                dve.memset(l_x[:, 0:3], 0.0).then_inc(lru_zero, 1)
                with dve.Fori(0, 8) as i:
                    u = layer * 8 + i

                    def hooks_c(g):
                        swa(u, i, g)
                        lru(u, i, g)
                    chunk(n0 + i + C0, hooks_c)
                dve.wait_ge(routed, layer * ROUTED + 16)
                dve.memset(d_q[0], 0.0)
                dve.memset(d_q[1], 0.0).then_inc(diff_zero, 1)
                with dve.Fori(0, 4) as i:

                    def hooks_d(g):
                        for h in range(2):
                            s = g - 8 * h
                            if 0 <= s < 8:
                                diff(layer * 8 + i * 2 + h, i * 2 + h, s)
                        if g == 4:
                            gate_mult_y(layer, i)
                    chunk(n0 + i + D0, hooks_d)
                with dve.Fori(0, 3) as i:
                    chunk(n0 + i + E0, lambda g: gate_mult_y(layer, i + 4) if g == 4 else None)
                chunk(n0 + O0, lambda g: gate_mult_y(layer, 7) if g == 4 else None,
                      before=lambda g: a_split_lo(layer * 2 + 1, g, Q_YS))
                with dve.Fori(0, 7) as i:
                    chunk(n0 + i + (O0 + 1), lambda g: add_x(layer, i) if g == 1 else None)
                add_x(layer, 7)

        @block.tensor
        def _(pe):
            def mm(out_, lhsT, rhs, start, stop):
                return pe.matmul(out_, lhsT, rhs, start=start, stop=stop, skip_group_check=True)

            def chunk(n, s, hooks=no_hooks):
                for g in range(NG):
                    pe.wait_ge(w_lo, n * NG + (g + 1 + RING))
                    pe.wait_ge(a_lo, s * NG + (g + 2))
                    slot = g % RING
                    for t in range(T):
                        if g == 0:
                            pe.wait_ge(main_free, n * T + (t + 1))
                        tt = slice(t * P, (t + 1) * P)
                        for k in range(KG):
                            kt = KG * g + k
                            mm(main[t][:, :], ahi[:, kt, tt], whi[:, slot, k, :], kt == 0, False)
                            mm(main[t][:, :], ahi[:, kt, tt], wlo[:, slot, k, :], False, False)
                            ins = mm(main[t][:, :], alo[:, kt, tt], whi[:, slot, k, :], False, kt == KT - 1)
                        if g == NG - 1 and t == 0:
                            ins.then_inc(main_ready, 1)
                    ins.then_inc(w_used, 1)
                    hooks(g)

            def turn_x(f, halves=(0, 1)):
                for half in halves:
                    pe.wait_ge(x_F, f * 2 + (half + 1))
                    for k in range(2):
                        for t in range(T):
                            if half == 0 and k == 0 and t == 0:
                                pe.wait_ge(x_added, f + 2)
                            c = 2 * half + k
                            ins = pe.transpose(M[half][:, (2 * k + t) * P:(2 * k + t + 1) * P],
                                               x_new[:, t, c * P:(c + 1) * P], ident[:, :])
                    ins.then_inc(x_T, 1)

            def gla(u, i, g):
                vcol = i * 2 * P
                if g == 2:
                    for t in range(T):
                        ins = mm(M[0][:, t * P:(t + 1) * P], g_aT[:, t * P:(t + 1) * P],
                                 g_wup[:, ds(i * P, P)], t == 0, True)
                    ins.then_inc(G["logit"], 1)
                if g == 5:
                    pe.wait_ge(G["g"], u + 1)
                    pe.wait_ge(G["y"], u + 1)
                    for t in range(T):
                        mm(M[1][:, t * P:(t + 1) * P], tri[:, :], g_g[:, t * P:(t + 1) * P], t == 0, True)
                        mm(M[1][:, 256 + t * P:256 + (t + 1) * P], suf[:, :], g_g[:, t * P:(t + 1) * P], False, True)
                        ins = mm(M[2][:, 2 * t:2 * t + 2], g_g[:, t * P:(t + 1) * P], chunk1[:, :], t == 0, True)
                    ins.then_inc(G["sums"], 1)
                if g == 8:
                    pe.wait_ge(G["qkd"], u + 1)
                    for t in range(T):
                        pe.transpose(M[3][:, t * P:(t + 1) * P], g_qd[:, t * P:(t + 1) * P], ident[:, :])
                        ins = pe.transpose(M[3][:, 256 + t * P:256 + (t + 1) * P], g_kd[:, t * P:(t + 1) * P],
                                           ident[:, :])
                    ins.then_inc(G["turned"], 1)
                    pe.wait_ge(G["kst"], u + 1)
                    for bank, off, t, c in ((4, 0, 0, 0), (4, 256, 0, 1), (5, 0, 1, 0)):
                        ins = mm(M[bank][:, off:off + 256], g_ks[:, t, c, :], Y[:, t, ds(vcol, 2 * P)], off == 0, True)
                    ins.then_inc(G["U"], 1)
                if g == 10:
                    pe.wait_ge(G["qkT"], u + 1)
                    for t in range(T):
                        for h in range(2):
                            b = 2 * t + h
                            ins = mm(M[0][:, b * P:(b + 1) * P], g_kT[:, t * P:(t + 1) * P],
                                     (g_q0, g_q1)[h][:, t * P:(t + 1) * P], b == 0, True)
                    ins.then_inc(G["AT"], 1)
                if g == 13:
                    pe.wait_ge(G["S"], u * 3 + 3)
                    for c in range(2):
                        r = slice(c * DK, (c + 1) * DK)
                        for t in range(T):
                            for h in range(2):
                                b = 2 * t + h
                                mm(M[1][r, b * P:(b + 1) * P], (g_q0, g_q1)[h][:, t * P + c * DK:t * P + (c + 1) * DK],
                                   g_S[:, 2 * t + c, :], b == 0, False)
                    pe.wait_ge(G["ATmasked"], u * 2 + 2)
                    for t in range(T):
                        for h in range(2):
                            b = 2 * t + h
                            ins = mm(M[1][:, b * P:(b + 1) * P], g_AT[:, b * P:(b + 1) * P],
                                     Y[:, t, ds(vcol + h * P, P)], False, True)
                    ins.then_inc(G["o"], 1)

            def swa(u, i, g):
                kv = (i // 4) * 256
                if g == 3:
                    pe.wait_ge(S["qn"], u + 1)
                    for t in range(T):
                        ins = pe.transpose(M[0][:, t * P:(t + 1) * P], s_qn[:, t * P:(t + 1) * P], ident[:, :])
                    ins.then_inc(S["turned"], 1)
                if g == 5:
                    pe.wait_ge(S["qT"], u + 1)
                    mm(M[1][:, 0:P], s_qT[:, 0:P], kT_swa[:, ds(kv, P)], True, True)
                    mm(M[1][:, P:3 * P], s_qT[:, P:2 * P], kT_swa[:, ds(kv, 2 * P)], False, True).then_inc(S["scores"], 1)
                if g == 8:
                    pe.wait_ge(S["p"], u + 1)
                    for b in range(3):
                        ins = pe.transpose(M[2][:, b * P:(b + 1) * P], s_p[:, b * P:(b + 1) * P], ident[:, :])
                    ins.then_inc(S["pT"], 1)
                if g == 10:
                    pe.wait_ge(S["pTc"], u + 1)
                    pe.wait_ge(S["y"], u + 1)
                    vc = (i // 4) * P + 2 * P
                    mm(M[3][:, 0:P], s_pT[:, 0:P], skv[:, 0, ds(vc, P)], True, True)
                    mm(M[3][:, P:2 * P], s_pT[:, P:2 * P], skv[:, 0, ds(vc, P)], False, False)
                    mm(M[3][:, P:2 * P], s_pT[:, 2 * P:3 * P], skv[:, 1, ds(vc, P)], False, True).then_inc(S["o"], 1)

            def lru(layer, u, i, g):
                if g == 3:
                    pe.wait_ge(L["rx"], u + 1)
                    for t in range(T):
                        ins = pe.transpose(M[4][:, t * P:(t + 1) * P], l_rx[:, t * P:(t + 1) * P], ident[:, :])
                    ins.then_inc(L["turned"], 1)
                if g == 6:
                    pe.wait_ge(L["xc"], u + 1)
                    pe.wait_ge(L["w_landed"], u * 32 + 32)
                    mm(M[5][:, 0:256], l_w[:, 0, :], l_xc, True, True)
                    mm(M[5][:, 256:512], l_w[:, 1, :], l_xc, False, True).then_inc(L["gates"], 1)
                if g == 11:
                    pe.wait_ge(L["h"], u + 1)
                    for t in range(T):
                        ins = pe.transpose(M[4][:, 256 + t * P:256 + (t + 1) * P], l_h[:, t * P:(t + 1) * P],
                                           ident[:, :])
                    ins.then_inc(L["hT"], 1)

            def diff(u, hcol, s):
                if s == 1:
                    pe.wait_ge(DF["qkn"], u + 1)
                    for t in range(T):
                        pe.transpose(M[0][:, t * P:(t + 1) * P], d_qn[:, t * P:(t + 1) * P], ident[:, :])
                        ins = pe.transpose(M[0][:, 256 + t * P:256 + (t + 1) * P], d_kn[:, t * P:(t + 1) * P],
                                           ident[:, :])
                    ins.then_inc(DF["turned"], 1)
                if s == 2:
                    pe.wait_ge(DF["qkT"], u + 1)
                    for c in range(2):
                        mm(M[1 + c][:, 0:P], d_q[c][:, 0:P], d_kT[:, 0:P], True, True)
                        ins = mm(M[1 + c][:, P:3 * P], d_q[c][:, P:2 * P], d_kT, False, True)
                    ins.then_inc(DF["scores"], 1)
                if s == 5:
                    pe.wait_ge(DF["w"], u + 1)
                    for b in range(3):
                        ins = pe.transpose(M[3][:, b * P:(b + 1) * P], d_w[:, b * P:(b + 1) * P], ident[:, :])
                    ins.then_inc(DF["wT"], 1)
                if s == 6:
                    pe.wait_ge(DF["wTc"], u + 1)
                    pe.wait_ge(DF["y"], u + 1)
                    mm(M[4][:, 0:P], d_wT[:, 0:P], dv[:, 0, ds(hcol, P)], True, True)
                    mm(M[4][:, P:2 * P], d_wT[:, P:2 * P], dv[:, 0, ds(hcol, P)], False, False)
                    mm(M[4][:, P:2 * P], d_wT[:, 2 * P:3 * P], dv[:, 1, ds(hcol, P)], False, True).then_inc(DF["o"], 1)

            def turn_gated(layer, j, g, hooks=(6, 9)):
                if g in hooks:
                    half = hooks.index(g)
                    pe.wait_ge(gate_mult, layer * 8 + (j + 1))
                    pe.wait_ge(gate_F, layer * 16 + (j * 2 + half + 1))
                    for k in range(2):
                        for t in range(T):
                            c = 2 * half + k
                            ins = pe.transpose(M[5][:, (2 * k + t) * P:(2 * k + t + 1) * P],
                                               stage[:, t, c * P:(c + 1) * P], ident[:, :])
                    ins.then_inc(gate_T, 1)

            pe.sem_inc(w_used, RING)
            pe.sem_inc(L["gates"], 1)
            pe.sem_inc(L["turned"], 1)
            pe.sem_inc(G["y"], 1)
            pe.sem_inc(S["y"], 1)
            pe.sem_inc(x_F, 2)
            pe.wait_ge(setup_in, N_SETUP * 16)
            pe.wait_ge(consts, 15 + HEADS)
            pe.transpose(M[0][:, 0:P], MIX[:, 0:P], ident[:, :])
            pe.transpose(M[1][:, 0:76], MIX[0:76, P:2 * P], ident[0:76, 0:76]).then_inc(par_turned, 1)
            pe.wait_ge(par_copied, 18)
            with pe.Fori(0, 8) as i:
                turn_x(i)
            with pe.Fori(0, DEPTH) as layer:
                n0 = layer * CHUNKS
                sx, sy = layer * 2, layer * 2 + 1
                with pe.Fori(0, 4) as i:
                    chunk(n0 + i, sx)
                pe.wait_ge(wa_lo_s, layer + 1)
                for t in range(T):
                    tt = slice(t * P, (t + 1) * P)
                    for k in range(KT):
                        o = M[0][:, t * RANK:(t + 1) * RANK]
                        mm(o, ahi[:, k, tt], wa_hi[:, k, :], k == 0, False)
                        mm(o, ahi[:, k, tt], wa_lo[:, k, :], False, False)
                        ins = mm(o, alo[:, k, tt], wa_hi[:, k, :], False, k == KT - 1)
                ins.then_inc(a_sum, 1)
                pe.wait_ge(a_ready, layer * 2 + 1)
                pe.wait_ge(gla_zero, layer + 1)
                for t in range(T):
                    ins = pe.transpose(M[1][0:RANK, t * P:(t + 1) * P], g_a[:, t, :], ident[:, :])
                ins.then_inc(a_T, 1)
                pe.wait_ge(a_ready, layer * 2 + 2)
                pe.wait_ge(a_up, layer * 32 + 32)
                pe.sem_inc(pe_passed, 1)
                with pe.Fori(0, 4) as i:
                    chunk(n0 + i + B0, sx, lambda g: gla(layer * 4 + i, i, g))
                pe.wait_ge(K["kn"], layer + 1)
                for b in range(4):
                    ins = pe.transpose(M[0][:, b * P:(b + 1) * P], cut(b * P, P), ident[:, :])
                ins.then_inc(K["turned"], 1)
                pe.wait_ge(K["kT"], layer + 1)
                pe.sem_inc(pe_passed, 1)
                with pe.Fori(0, 8) as i:
                    u = layer * 8 + i

                    def hooks_c(g):
                        swa(u, i, g)
                        lru(layer, u, i, g)
                    chunk(n0 + i + C0, sx, hooks_c)
                with pe.Fori(0, 4) as i:

                    def hooks_d(g):
                        for h in range(2):
                            s = g - 8 * h
                            if 0 <= s < 8:
                                diff(layer * 8 + i * 2 + h, i * 2 * P + h * P, s)
                        turn_gated(layer, i, g)
                    chunk(n0 + i + D0, sx, hooks_d)
                with pe.Fori(0, 3) as i:
                    chunk(n0 + i + E0, sx, lambda g: turn_gated(layer, i + 4, g))
                chunk(n0 + O0, sy, lambda g: turn_gated(layer, 7, g))
                with pe.Fori(0, 7) as i:
                    chunk(n0 + i + (O0 + 1), sy, lambda g: turn_x(layer * 8 + i + 8, (g - 5,)) if g in (5, 6) else None)
                turn_x(layer * 8 + 15)


_INS = ['x', 'norm_w', 'w_in', 'w_out', 'gla_w_up', 'gla_b_up', 'gla_norm_w', 'swa_q_norm', 'swa_k_norm',
        'swa_sinks', 'diff_q_norm', 'diff_k_norm', 'diff_lq1', 'diff_lk1', 'diff_lq2', 'diff_lk2',
        'diff_out_norm', 'lru_conv_w', 'lru_conv_b', 'lru_w_r', 'lru_b_r', 'lru_w_i', 'lru_b_i', 'lru_lambda']


def kernel(**inputs):
    import numpy as _np
    import concourse.bacc as _bacc
    from concourse import mybir as _mybir
    from concourse.bass_utils import run_bass_kernel_spmd as _run

    nc = _bacc.Bacc("TRN2", target_bir_lowering=False, num_devices=1)
    arrays, args = {}, []
    for name in _INS:
        a = _np.ascontiguousarray(inputs[name])
        arrays[f"in_{name}"] = a
        args.append(nc.dram_tensor(f"in_{name}", a.shape, _mybir.dt.from_np(a.dtype), kind="ExternalInput").ap())
    shape = inputs['x'].shape
    args.append(nc.dram_tensor("out", shape, _mybir.dt.from_np(_np.dtype('float32')), kind="ExternalOutput").ap())
    hybrid_trunk(nc, *args)
    r = _run(nc, [arrays], core_ids=[0])
    return r.results[0]["out"]
```

```python
import math
from contextlib import ExitStack

import concourse.bass as bass
from concourse import mybir

F32 = mybir.dt.float32
F32R = mybir.dt.float32r
ALU = mybir.AluOpType
ACT = mybir.ActivationFunctionType
AX = mybir.AxisListType

P = 128


def hybrid_trunk(nc, x, norm_w, w_in, w_out, gla_w_up, gla_b_up, gla_norm_w,
                 swa_q_norm, swa_k_norm, swa_sinks, diff_q_norm, diff_k_norm,
                 diff_lq1, diff_lk1, diff_lq2, diff_lk2, diff_out_norm,
                 lru_conv_w, lru_conv_b, lru_w_r, lru_b_r, lru_w_i, lru_b_i, lru_lambda, out):
    DEPTH, D, D_IN = w_in.shape
    SEQ = x.shape[1]
    T = SEQ // P
    KT = D // P
    NC = 512
    KG = 2
    NG = KT // KG
    RING = 4
    RANK = gla_w_up.shape[1]
    BW = D // 4
    DK = 64
    HEADS = BW // P
    GLA_QK = HEADS * DK
    EPS = 1e-6
    TAU = 16.0
    MASKED = 1e30
    assert (T, KT, NG, HEADS) == (2, 32, 16, 8)

    C_GLA = 0
    C_A = 2 * GLA_QK + BW
    C_SWA = C_A + RANK
    C_DIFF = C_SWA + BW + 2 * 2 * P
    C_RX = C_DIFF + 3 * BW
    C_GATE = C_RX + BW
    assert C_GATE + D == D_IN

    A0, B0, C0, D0, E0, O0, CHUNKS = 0, 4, 8, 16, 20, 23, 31
    N_SETUP = 14 + 5 * DEPTH
    ROUTED = 15

    DIFF_PE = ({0: "turn", 1: "scores", 5: "wT", 6: "o"}, {7: "turn", 8: "scores", 12: "wT", 13: "o"})
    DIFF_ACT = ({3: "turned", 6: "exp", 9: "out"}, {10: "turned", 12: "exp", 15: "out"})
    DIFF_DVE = ({4: "scores", 6: "w", 7: "wT"}, {11: "scores", 12: "w", 14: "wT"})

    Q_NORM, Q_LRU, Q_SQ, Q_SK, Q_DQ, Q_DK, Q_LAM, Q_YS, Q_SINK, Q_SLOPE, NQ = \
        0, 32, 104, 105, 106, 107, 108, 112, 144, 152, 160

    ctx = ExitStack()
    with ctx:
        def sb(name, shape, dt=F32):
            return ctx.enter_context(nc.sbuf_tensor(name, shape, dt))

        def sem(name):
            return ctx.enter_context(nc.semaphore(name))

        ahi = sb("act_hi", [P, KT, SEQ], F32R)
        alo = sb("act_lo", [P, KT, SEQ], F32R)
        F = sb("act_T", [P, KT * SEQ])
        Y = sb("mix_Y", [P, T, D])
        raw = sb("w_raw", [P, RING, KG, NC])
        whi = sb("w_hi", [P, RING, KG, NC], F32R)
        wlo = sb("w_lo", [P, RING, KG, NC], F32R)
        stage = sb("stage", [P, T, NC])
        wa_hi = sb("wa_hi", [P, KT, RANK], F32R)
        wa_lo = sb("wa_lo", [P, KT, RANK], F32R)
        ident = sb("ident", [P, P])
        tri = sb("tri", [P, P])
        suf = sb("suf", [P, P])
        chunk1 = sb("chunk1", [P, 2])
        dist = sb("dist", [P, 3 * P])
        par = sb("par", [P, DEPTH, NQ])
        pc = sb("par_now", [P, NQ])
        rstd = sb("rstd", [P, T])
        ssq = sb("ssq", [P, T, 8])
        dist_swa = sb("dist_swa", [P, 3 * P])
        small = sb("small", [P, 64])
        cst = sb("cst", [P, 4])
        one, eps, tiny = cst[:, 0:1], cst[:, 1:2], cst[:, 2:3]
        MIX = sb("mix", [P, 4352])

        gq = F[:, 0:1024].rearrange("p (t n) -> p t n", t=T)
        gk = F[:, 1024:2048].rearrange("p (t n) -> p t n", t=T)
        kT_swa = F[:, 2048:2560]
        skv = F[:, 3072:4096].rearrange("p (t n) -> p t n", t=T)
        dk = F[:, 4096:6144].rearrange("p (t n) -> p t n", t=T)
        dv = F[:, 6144:8192].rearrange("p (t n) -> p t n", t=T)

        def cut(base, size):
            return MIX[:, base:base + size]

        g_e, g_l1, g_g = cut(0, 256), cut(256, 256), cut(512, 256)
        g_eb, g_enb, g_es = cut(768, 256), cut(1024, 256), cut(1280, 256)
        g_qd, g_kd = cut(1536, 256), cut(1792, 256)
        g_ks = F[:, 4096:4608].rearrange("p (t c n) -> p t c n", t=T, c=2)
        g_q0, g_q1, g_kT = F[:, 4608:4864], F[:, 4864:5120], F[:, 5120:5376]
        g_S = F[:, 5376:5888].rearrange("p (k n) -> p k n", k=4)
        g_AT = F[:, 5888:6400]
        g_dec = F[:, 6400:6404]
        g_rs = F[:, 6404:6412]
        g_sq = cut(2048, 512)
        inv_rms = cut(2560, T * (RANK + 1)).rearrange("p (t n) -> p t n", t=T)
        g_aT = MIX[0:RANK + 1, 2688:2944]
        g_wup = MIX[0:RANK + 1, 3072:3584]
        wa_raw = cut(3584, KT * RANK).rearrange("p (k n) -> p k n", k=KT)

        s_qn, s_qT = cut(0, 256), cut(256, 256)
        s_s, s_p, s_pT = cut(512, 384), cut(896, 384), cut(1280, 384)
        s_sm = small[:, 0:16]
        s_sq = cut(1664, 256)
        l_x = cut(1920, 260)
        l_xc = cut(2180, 256)
        l_ri = cut(2436, 512)
        l_t, l_a = F[:, 0:256], F[:, 256:512]
        l_l2, l_l1, l_u = F[:, 512:768], F[:, 768:1024], F[:, 1024:1280]
        l_h = F[:, 1280:1536]
        l_rx = F[:, 1536:1792]
        l_w = F[:, 2560:2816].rearrange("p (r n) -> p r n", r=2)
        l_par = small[:, 16:25]
        d_sq = cut(0, 512)
        d_qn, d_kn = cut(512, 256), cut(768, 256)
        d_q = (cut(1024, 256), cut(1280, 256))
        d_kT = cut(1536, 256)
        d_s = cut(1792, 768)
        d_p = cut(2560, 768)
        d_w, d_wT = cut(3328, 384), cut(3712, 384)
        d_osq = cut(4096, 256)
        d_sm = small[:, 32:64]
        x_old = cut(0, 1024).rearrange("p (t n) -> p t n", t=T)
        x_new = cut(1024, 1024).rearrange("p (t n) -> p t n", t=T)
        x_sq = cut(2048, 512)

        main = [ctx.enter_context(nc.psum_tensor(f"main{t}", [P, NC], F32)) for t in range(T)]
        M = [ctx.enter_context(nc.psum_tensor(f"mixer{k}", [P, NC], F32)) for k in range(6)]

        setup_in = sem("setup_in")
        consts = sem("consts")
        par_turned = sem("par_turned")
        par_copied = sem("par_copied")
        par_math = sem("par_math")
        par_act = sem("par_act")
        now_ready = sem("now_ready")
        w_landed = [sem(f"w_landed{s}") for s in range(RING // 2)]
        w_hi = sem("w_hi_ready")
        w_lo = sem("w_lo_ready")
        w_used = sem("w_used")
        a_hi = sem("act_hi_ready")
        a_lo = sem("act_lo_ready")
        main_ready = sem("main_ready")
        main_free = sem("main_free")
        pool_passed, pe_passed = sem("pool_passed"), sem("pe_passed")
        routed = sem("routed")
        wa_landed, wa_hi_s, wa_lo_s = sem("wa_landed"), sem("wa_hi_ready"), sem("wa_lo_ready")
        gate_mult = sem("gate_mult")
        gate_T, gate_F = sem("gate_turned"), sem("gate_copied")
        gla_zero, lru_zero, diff_zero = sem("gla_zero"), sem("lru_zero"), sem("diff_zero")
        a_sum, a_ready, a_up = sem("a_summed"), sem("a_ready"), sem("a_up")
        inv_zero, inv_ready = sem("inv_zero"), sem("inv_ready")
        G = {n: sem("gla_" + n) for n in
             "logit e l1 min g sums exps dec qkd kst turned U qkT S AT ATcopied ATmasked o sq ssq ln rstd y".split()}
        S = {n: sem("swa_" + n) for n in
             "par sq ssq ln rstd qn turned qT scores s max neg p sink den rden pT pTc o y".split()}
        K = {n: sem("swak_" + n) for n in "ssq ln rstd kn turned kT".split()}
        L = {n: sem("lru_" + n) for n in
             "par rx w_landed turned x c0 c1 c2 xc gates r i t a ln2 ln1 d ix sf u h hT y".split()}
        DF = {n: sem("diff_" + n) for n in
              "par ssq sqk ln rstd qkn turned qkT scores s max neg p rp coef w0 w wT wTc o osq oln orstd y".split()}
        x_in = [sem(f"x_in{i}") for i in range(4)]
        x_squared_in = sem("x_squared_in")
        x_loaded, x_added, x_stored = sem("x_loaded"), sem("x_added"), sem("x_stored")
        x_squared, x_T, x_F = sem("x_squared"), sem("x_turned"), sem("x_copied")
        rs_sum, rs_ln, rs_ready = sem("rs_sum"), sem("rs_ln"), sem("rs_ready")

        block = ctx.enter_context(nc.Block())

        def ds(i, n):
            return bass.ds(i, n)

        def no_hooks(g):
            pass

        @block.sync
        def _(sp):
            def weight_chunk(n, src):
                for g in range(NG):
                    sp.wait_ge(w_lo, n * NG + (g + 1))
                    sp.dma_start(raw[:, g % RING, :, :], src(g)).then_inc(w_landed[g % RING // 2], 16)

            def from_in(layer, col):
                return lambda g: w_in[layer, g * KG * P:(g + 1) * KG * P, ds(col, NC)].rearrange(
                    "(k p) n -> p k n", p=P)

            for i in range(4):
                cols = slice(i * BW, (i + 1) * BW)
                sp.dma_start(Y[:, :, cols], x[0, :, cols].rearrange("(t p) n -> p t n", p=P)
                             ).then_inc(x_in[i], 16)
            with sp.Fori(0, DEPTH) as layer:
                n0 = layer * CHUNKS
                for first, count, col in ((0, 4, C_GLA), (4, 3, C_SWA), (7, 2, C_RX),
                                          (9, 6, C_DIFF), (15, 8, C_GATE)):
                    with sp.Fori(0, count) as i:
                        weight_chunk(n0 + i + first, from_in(layer, i * NC + col))
                with sp.Fori(0, 8) as i:
                    weight_chunk(n0 + i + O0, lambda g: w_out[
                        layer, g * KG * P:(g + 1) * KG * P, ds(i * NC, NC)].rearrange(
                            "(k p) n -> p k n", p=P))
            sp.wait_ge(x_stored, 16 * 8 * (DEPTH + 1))

        @block.gpsimd
        def _(pool):
            def after(semaphore, value):
                pool.wait_ge(semaphore, value)
                pool.sem_inc(pool_passed, 1)

            pool.memset(ident[:, :], 0.0).then_inc(consts, 1)
            pool.memset(tri[:, :], 1.0 / TAU).then_inc(consts, 1)
            pool.memset(suf[:, :], 1.0 / TAU).then_inc(consts, 1)
            pool.memset(chunk1[:, :], 0.0).then_inc(consts, 1)
            pool.iota(dist[:, 0:P], pattern=[[-1, P]], base=0, channel_multiplier=1,
                      allow_small_or_imprecise_dtypes=True).then_inc(consts, 1)
            pool.iota(dist[:, P:3 * P], pattern=[[-1, 2 * P]], base=P, channel_multiplier=1,
                      allow_small_or_imprecise_dtypes=True).then_inc(consts, 1)
            pool.memset(par[:, :, Q_LAM + 1:Q_YS], 0.0)
            for h in range(HEADS):
                pool.memset(par[:, :, Q_SLOPE + h:Q_SLOPE + h + 1], -2.0 ** -(h + 1.0)).then_inc(consts, 1)
            pool.wait_ge(consts, 6 + HEADS)
            pool.affine_select(out=ident[:, :], in_=ident[:, :], compare_op=ALU.not_equal, fill=1.0,
                               base=0, pattern=[[-1, P]], channel_multiplier=1).then_inc(consts, 1)
            pool.affine_select(out=tri[:, :], in_=tri[:, :], compare_op=ALU.is_ge, fill=0.0,
                               base=0, pattern=[[1, P]], channel_multiplier=-1).then_inc(consts, 1)
            pool.affine_select(out=suf[:, :], in_=suf[:, :], compare_op=ALU.is_gt, fill=0.0,
                               base=0, pattern=[[-1, P]], channel_multiplier=1).then_inc(consts, 1)
            pool.affine_select(out=dist[:, 0:P], in_=dist[:, 0:P], compare_op=ALU.is_ge, fill=MASKED,
                               base=0, pattern=[[-1, P]], channel_multiplier=1).then_inc(consts, 1)
            pool.affine_select(out=dist[:, P:3 * P], in_=dist[:, P:3 * P], compare_op=ALU.is_ge,
                               fill=MASKED, base=P, pattern=[[-1, 2 * P]],
                               channel_multiplier=1).then_inc(consts, 1)
            pool.wait_ge(consts, 11 + HEADS)
            pool.memset(tri[0:DK, DK:P], 0.0).then_inc(consts, 1)
            pool.memset(suf[DK:P, 0:DK], 0.0).then_inc(consts, 1)
            for c in range(2):
                pool.memset(chunk1[c * DK:(c + 1) * DK, c:c + 1], 1.0 / TAU).then_inc(consts, 1)

            def load_x(f, i):
                after(x_added, f + 1)
                pool.dma_start(x_old, out[0, :, ds(i * NC, NC)].rearrange("(t p) n -> p t n", p=P)
                               ).then_inc(x_loaded, 16)

            def store_x(f, i):
                after(x_added, f + 2)
                pool.dma_start(out[0, :, ds(i * NC, NC)].rearrange("(t p) n -> p t n", p=P), x_new
                               ).then_inc(x_stored, 16)

            pool.sem_inc(routed, 1)
            for i in range(4):
                pool.wait_ge(x_in[i], 16)
            with pool.Fori(0, 8) as i:
                pool.dma_start(out[0, :, ds(i * NC, NC)].rearrange("(t p) n -> p t n", p=P),
                               Y[:, :, ds(i * NC, NC)]).then_inc(x_stored, 16)

            def route(layer, j, dst):
                after(main_free, (layer * CHUNKS + j + 2) * T)
                pool.tensor_copy(dst, stage[:, :, :]).then_inc(routed, 1)

            def hand_rx(layer, n):
                u = layer * 8 + n
                after(routed, layer * ROUTED + n + 9)
                after(L["turned"], u + 1)
                pool.tensor_copy(l_rx.rearrange("p (t n) -> p t n", t=T),
                                 Y[:, :, ds(n * P + 3 * BW, P)]).then_inc(L["rx"], 1)

            def mask_intra(layer, i):
                u = layer * 4 + i
                AT = g_AT.rearrange("p (u i) -> p u i", u=4)
                after(G["ATcopied"], u + 1)
                pool.affine_select(out=AT, in_=AT, compare_op=ALU.is_ge, fill=0.0, base=0,
                                   pattern=[[0, 4], [1, P]], channel_multiplier=-1).then_inc(G["ATmasked"], 1)
                after(G["ATmasked"], u * 2 + 1)
                pool.memset(AT[0:DK, :, DK:P], 0.0).then_inc(G["ATmasked"], 1)

            with pool.Fori(0, DEPTH) as layer:
                pool.dma_start(g_wup[0:RANK, :], gla_w_up[layer, :, :]).then_inc(a_up, 16)
                pool.dma_start(g_wup[RANK:RANK + 1, :],
                               gla_b_up[ds(layer, 1), :]).then_inc(a_up, 16)
                pool.dma_start(wa_raw, w_in[layer, :, C_A:C_A + RANK].rearrange(
                    "(k p) n -> p k n", p=P)).then_inc(wa_landed, 16)
                after(a_lo, layer * 2 * NG + (NG + 1))
                route(layer, 0, gq)
                route(layer, 1, gk)
                after(x_stored, layer * 128 + 128)
                with pool.Fori(0, 2) as i:
                    route(layer, i + 2, Y[:, :, ds(i * NC, NC)])
                with pool.Fori(0, 2) as i:
                    mask_intra(layer, i)
                    route(layer, i + 4, Y[:, :, ds(i * NC + BW, NC)])
                mask_intra(layer, 2)
                route(layer, 6, skv)
                mask_intra(layer, 3)
                for first, dst in ((0, lambda i: Y[:, :, ds(i * NC + 3 * BW, NC)]),
                                   (2, lambda i: Y[:, :, ds(i * NC + 2 * BW, NC)]),
                                   (4, lambda i: dk[:, :, ds(i * NC, NC)]),
                                   (6, lambda i: dv[:, :, ds(i * NC, NC)])):
                    if first == 4:
                        after(G["y"], layer * 4 + 5)
                    with pool.Fori(0, 2) as i:
                        route(layer, i + 7 + first, dst(i))
                        hand_rx(layer, i + first)
                after(DF["y"], layer * 8 + 9)
                with pool.Fori(0, 8) as i:
                    f = layer * 8 + i + 8
                    after(x_stored, layer * 128 + i * 16 + 16)
                    load_x(f, i)
                    store_x(f, i)

        @block.scalar
        def _(act):
            def a_split_hi(s, g, first, scale, ready, base):
                act.wait_ge(ready, base)
                for k in range(KG * g, KG * g + KG):
                    ins = act.activation(ahi[:, k, :], F[:, k * SEQ:(k + 1) * SEQ], ACT.Copy,
                                         scale=pc[:, scale + k:scale + k + 1])
                ins.then_inc(a_hi, 1)

            def chunk(n, hooks=no_hooks, split=None):
                for g in range(NG):
                    if g % 2 == 0:
                        act.wait_ge(w_landed[g % RING // 2], n * (32 * (NG // RING)) + 32 * (g // RING + 1))
                        act.wait_ge(w_used, n * NG + (g + 2))
                    act.activation(whi[:, g % RING, :, :], raw[:, g % RING, :, :], ACT.Copy).then_inc(w_hi, 1)
                    hooks(g)
                    if split and g >= 1:
                        for k in ((0, 1) if g == 1 else (g,)):
                            split(k)

            def evac(n, func):
                act.wait_ge(main_ready, n + 1)
                act.activation(stage[:, 0, :], main[0][:, :], func, scale=rstd[:, 0:1]).then_inc(main_free, 1)
                act.wait_ge(w_used, n * NG + (NG + RING))
                act.activation(stage[:, 1, :], main[1][:, :], func, scale=rstd[:, 1:2]).then_inc(main_free, 1)

            def evac_raw(layer, j):
                act.wait_ge(routed, layer * ROUTED + (j + 1))
                evac(layer * CHUNKS + j, ACT.Copy)

            def evac_gate(layer, j):
                act.wait_ge(gate_F, layer * 16 + (j * 2 + 1))
                act.wait_ge(routed, layer * ROUTED + (ROUTED + 1))
                evac(layer * CHUNKS + j + ROUTED, ACT.Silu)
                act.preload_act_table_set("natural_log_exp_and_others")

            def rsqrt(dst, src, n, ln, done, u):
                act.activation(dst, src, ACT.Ln, scale=1.0 / n, bias=eps[:, :]).then_inc(ln, 1)
                act.wait_ge(ln, u)
                act.activation(dst, dst, ACT.Exp, scale=-0.5).then_inc(done, 1)

            def gla(u, g):
                if g == 4:
                    act.wait_ge(G["logit"], u + 1)
                    for t in range(T):
                        ins = act.activation(g_e[:, t * P:(t + 1) * P], M[0][:, t * P:(t + 1) * P], ACT.Abs,
                                             scale=rstd[:, t:t + 1])
                    ins.then_inc(G["e"], 1)
                    act.wait_ge(G["e"], u * 2 + 1)
                    act.activation(g_e, g_e, ACT.Exp, scale=-1.0).then_inc(G["e"], 1)
                    act.wait_ge(G["e"], u * 2 + 2)
                    act.activation(g_l1, g_e, ACT.Ln, bias=one[:, :]).then_inc(G["l1"], 1)
                if g == 6:
                    act.wait_ge(G["sums"], u + 1)
                    act.activation(g_eb, M[1][:, 0:256], ACT.Exp)
                    act.activation(g_enb, M[1][:, 0:256], ACT.Exp, scale=-1.0)
                    act.activation(g_es, M[1][:, 256:512], ACT.Exp).then_inc(G["exps"], 1)
                    act.activation(g_dec, M[2][:, 0:4], ACT.Exp).then_inc(G["dec"], 1)
                if g == 10:
                    act.wait_ge(G["turned"], u + 1)
                    act.activation(g_q0[0:DK, :], M[3][0:DK, 0:256], ACT.Copy)
                    act.activation(g_q1[DK:P, :], M[3][DK:P, 0:256], ACT.Copy)
                    act.activation(g_kT, M[3][:, 256:512], ACT.Copy).then_inc(G["qkT"], 1)
                if g == 15:
                    act.wait_ge(G["o"], u + 1)
                    act.activation(g_sq, M[1][:, :], ACT.Square).then_inc(G["sq"], 1)
                    act.wait_ge(G["ssq"], u + 1)
                    rsqrt(g_rs[:, 4:8], g_rs[:, 0:4], P, G["ln"], G["rstd"], u + 1)

            def swa(u, g):
                if g == 1:
                    act.wait_ge(S["ssq"], u + 1)
                    rsqrt(s_sm[:, 2:4], s_sm[:, 0:2], P, S["ln"], S["rstd"], u + 1)
                if g == 7:
                    act.wait_ge(S["turned"], u + 1)
                    act.activation(s_qT, M[0][:, 0:256], ACT.Copy, scale=pc[:, Q_SQ:Q_SQ + 1]).then_inc(S["qT"], 1)
                if g == 10:
                    act.wait_ge(S["neg"], u + 1)
                    act.activation(s_p[:, 0:P], s_s[:, 0:P], ACT.Exp, bias=s_sm[:, 6:7],
                                   accum_out=s_sm[:, 8:9])
                    act.activation(s_p[:, P:3 * P], s_s[:, P:3 * P], ACT.Exp, bias=s_sm[:, 7:8],
                                   accum_out=s_sm[:, 9:10]).then_inc(S["p"], 1)
                    act.activation(s_sm[:, 10:12], s_sm[:, 6:8], ACT.Exp, bias=s_sm[:, 14:15]).then_inc(S["sink"], 1)
                
            def lru(layer, u, i, g):
                if g == 0:
                    act.wait_ge(L["gates"], u + 1)
                    act.dma_start(l_w[:, 0, :], lru_w_r[layer, ds(i, 1), :, :].rearrange(
                        "b i j -> i (b j)")).then_inc(L["w_landed"], 16)
                    act.dma_start(l_w[:, 1, :], lru_w_i[layer, ds(i, 1), :, :].rearrange(
                        "b i j -> i (b j)")).then_inc(L["w_landed"], 16)
                if g == 10:
                    act.wait_ge(L["gates"], u + 2)
                    act.activation(l_ri[:, 0:256], M[5][:, 0:256], ACT.Sigmoid, bias=l_par[:, 5:6]).then_inc(L["r"], 1)
                    act.activation(l_ri[:, 256:512], M[5][:, 256:512], ACT.Sigmoid,
                                   bias=l_par[:, 6:7]).then_inc(L["i"], 1)
                if g == 11:
                    act.wait_ge(L["r"], u + 1)
                    act.activation(l_t, l_ri[:, 0:256], ACT.Tanh, scale=l_par[:, 7:8],
                                   bias=tiny[:, :]).then_inc(L["t"], 1)
                    act.preload_act_table_set("natural_log_exp_and_others")
                    act.activation(l_a, l_ri[:, 0:256], ACT.Exp, scale=l_par[:, 8:9]).then_inc(L["a"], 1)
                if g == 12:
                    act.wait_ge(L["t"], u + 1)
                    act.activation(l_l2, l_t, ACT.Ln, scale=2.0)
                    act.activation(l_l1, l_t, ACT.Ln, bias=one[:, :]).then_inc(L["ln1"], 1)
                if g == 13:
                    act.wait_ge(L["d"], u + 1)
                    act.activation(l_l2, l_l2, ACT.Exp, scale=0.5).then_inc(L["sf"], 1)

            def diff(u, col, s):
                if s == "norm":
                    act.wait_ge(DF["ssq"], u + 1)
                    rsqrt(d_sm[:, 8:16], d_sm[:, 0:8], DK, DF["ln"], DF["rstd"], u + 1)
                if s == "turned":
                    act.wait_ge(DF["turned"], u + 1)
                    act.activation(d_q[0][0:DK, :], M[0][0:DK, 0:256], ACT.Copy, scale=pc[0:DK, Q_DQ:Q_DQ + 1])
                    act.activation(d_q[1][DK:P, :], M[0][DK:P, 0:256], ACT.Copy, scale=pc[DK:P, Q_DQ:Q_DQ + 1])
                    act.activation(d_kT, M[0][:, 256:512], ACT.Copy, scale=pc[:, Q_DK:Q_DK + 1]).then_inc(DF["qkT"], 1)
                if s == "exp":
                    act.wait_ge(DF["neg"], u + 1)
                    for c in range(2):
                        b = c * 384
                        act.activation(d_p[:, b:b + P], d_s[:, b:b + P], ACT.Exp,
                                       bias=d_sm[:, 20 + c:21 + c], accum_out=d_sm[:, 24 + c:25 + c])
                        ins = act.activation(d_p[:, b + P:b + 384], d_s[:, b + P:b + 384], ACT.Exp,
                                             bias=d_sm[:, 22 + c:23 + c], accum_out=d_sm[:, 26 + c:27 + c])
                    ins.then_inc(DF["p"], 1)
                if s == "out":
                    act.wait_ge(DF["o"], u + 1)
                    for t in range(T):
                        ins = act.activation(d_osq[:, t * P:(t + 1) * P], M[4][:, t * P:(t + 1) * P], ACT.Square,
                                             accum_out=small[:, 26 + t:27 + t])
                    ins.then_inc(DF["osq"], 1)
                    act.wait_ge(DF["osq"], u + 1)
                    rsqrt(small[:, 28:30], small[:, 26:28], P, DF["oln"], DF["orstd"], u + 1)
                    act.wait_ge(DF["orstd"], u + 1)
                    for t in range(T):
                        ins = act.activation(Y[:, t, ds(col, P)], M[4][:, t * P:(t + 1) * P], ACT.Copy,
                                             scale=small[:, 28 + t:29 + t])
                    ins.then_inc(DF["y"], 1)

            def gate_out(layer, j, g, hooks=(8, 10)):
                if g in hooks:
                    half = hooks.index(g)
                    act.wait_ge(gate_T, layer * 16 + (j * 2 + half + 1))
                    act.activation(F[:, ds(j * 1024 + half * 512, 512)], M[5][:, :], ACT.Copy).then_inc(gate_F, 1)

            def square_x(f, i):
                act.wait_ge(x_added, f + 2)
                for t in range(T):
                    act.wait_ge(x_squared, f * T + (t + 1))
                    act.activation(x_sq, x_new[:, t, :], ACT.Square,
                                   accum_out=ssq[:, t, ds(i, 1)]).then_inc(x_squared, 1)

            def copy_x(f, i, half):
                act.wait_ge(x_T, f * 2 + half + 1)
                act.activation(F[:, ds(i * 1024 + half * 512, 512)], M[half][:, :], ACT.Copy).then_inc(x_F, 1)

            def finish_x(f, i):
                square_x(f, i)
                for half in range(2):
                    copy_x(f, i, half)

            act.preload_act_table_set("natural_log_exp_and_others")
            act.sem_inc(main_free, T)
            act.sem_inc(gate_F, 1)
            act.sem_inc(x_squared, 1)
            act.sem_inc(DF["y"], 1)
            r1, r2 = MIX[:, 0:128], MIX[0:76, 128:256]
            row = 0

            def rows(dst, src):
                act.dma_start(dst, src).then_inc(setup_in, 16)

            rows(r1[0:64, :], norm_w.rearrange("l (k p) -> (l k) p", p=P))
            rows(r1[64:128, :], lru_conv_w.rearrange("l w (n p) -> (l w n) p", p=P))
            for q, src in enumerate((lru_conv_b, lru_b_r, lru_b_i, lru_lambda)):
                rows(r2[16 * q:16 * q + 16, :], src.rearrange("l (n p) -> (l n) p", p=P))
            for q, src in enumerate((gla_norm_w, swa_q_norm, swa_k_norm, diff_out_norm)):
                rows(r2[64 + 2 * q:66 + 2 * q, :], src)
            for q, src in enumerate((diff_q_norm, diff_k_norm)):
                for c in range(2):
                    rows(r2[72 + 2 * q:74 + 2 * q, c * DK:(c + 1) * DK], src)
            for l in range(DEPTH):
                rows(par[:, l, Q_SINK:Q_SINK + HEADS], swa_sinks[l, :].partition_broadcast(P))
                for q, src in enumerate((diff_lq1, diff_lk1, diff_lq2, diff_lk2)):
                    rows(cut(512 + (4 * l + q) * DK, DK), src[l, :].partition_broadcast(P))
            def copy_input(q):
                act.wait_ge(x_T, q + 1)
                act.activation(F[:, q * NC:(q + 1) * NC], M[2 + q % 4][:, :], ACT.Copy).then_inc(x_F, 1)

            for q in range(NG // 2):
                copy_input(q)
            act.wait_ge(par_math, 5)
            act.activation(small[:, 0:4], small[:, 0:4], ACT.Exp).then_inc(par_act, 1)
            act.wait_ge(par_math, 6)
            act.activation(cut(1600, 16), cut(1600, 16), ACT.Exp, scale=-1.0).then_inc(par_act, 1)
            for q in range(NG // 2, NG):
                copy_input(q)

            with act.Fori(0, DEPTH) as layer:
                n0 = layer * CHUNKS

                def split_x(g):
                    if g == 0:
                        act.wait_ge(now_ready, layer + 1)
                        act.wait_ge(w_used, n0 * NG + RING)
                    a_split_hi(layer * 2, g, 0, Q_NORM, x_F, layer * 16 + (g + 3))

                def split_y(g):
                    if g == 0:
                        act.wait_ge(w_used, n0 * NG + O0 * NG + RING)
                    a_split_hi(layer * 2 + 1, g, 0, Q_YS, gate_F, layer * 16 + (g + 2))

                def hooks_first(g):
                    if g == 5:
                        act.wait_ge(rs_sum, layer + 1)
                        rsqrt(rstd[:, :], small[:, 30:32], D, rs_ln, rs_ready, layer + 1)
                    if g == 7:
                        act.wait_ge(wa_landed, layer * 16 + 16)
                        act.activation(wa_hi[:, :, :], wa_raw, ACT.Copy).then_inc(wa_hi_s, 1)
                chunk(n0, hooks_first, split=split_x)
                with act.Fori(0, 3) as i:
                    chunk(n0 + i + 1, lambda g: evac_raw(layer, i) if g == 1 else None)
                act.wait_ge(x_stored, layer * 128 + 128)
                act.wait_ge(a_sum, layer + 1)
                act.activation(g_aT, M[1][0:RANK + 1, 0:256], ACT.Copy).then_inc(a_ready, 1)
                act.wait_ge(gla_zero, layer + 1)
                with act.Fori(0, 4) as i:

                    def hooks_b(g):
                        if g == 1:
                            evac_raw(layer, i + 3)
                        gla(layer * 4 + i, g)
                    chunk(n0 + i + B0, hooks_b)
                act.wait_ge(K["ssq"], layer + 1)
                rsqrt(s_sm[:, 4:8], s_sm[:, 0:4], P, K["ln"], K["rstd"], layer + 1)
                act.wait_ge(K["turned"], layer + 1)
                act.activation(kT_swa, M[0][:, :], ACT.Copy, scale=pc[:, Q_SK:Q_SK + 1]).then_inc(K["kT"], 1)
                with act.Fori(0, 8) as i:
                    u = layer * 8 + i

                    def hooks_c(g):
                        if g == 1:
                            evac_raw(layer, i + 7)
                        swa(u, g)
                        lru(layer, u, i, g)
                    chunk(n0 + i + C0, hooks_c)
                diff(layer * 8, 0, "norm")
                def hooks_d(i, g, last=False):
                    if g == 1:
                        evac_gate(layer, i)
                    for h in range(2):
                        diff(layer * 8 + i * 2 + h, i * 2 * P + (h * P + 2 * BW),
                             DIFF_ACT[h].get(g))
                    if g in (4, 14) and not (last and g == 14):
                        diff(layer * 8 + i * 2 + (1 if g == 4 else 2), 0, "norm")
                    gate_out(layer, i, g)

                with act.Fori(0, 3) as i:
                    chunk(n0 + i + D0, lambda g: hooks_d(i, g))
                chunk(n0 + D0 + 3, lambda g: hooks_d(3, g, last=True))
                with act.Fori(0, 3) as i:

                    def hooks_e(g):
                        if g == 1:
                            evac_gate(layer, i + 4)
                        gate_out(layer, i + 4, g)
                    chunk(n0 + i + E0, hooks_e)

                def hooks_o(g):
                    if g == 1:
                        evac_gate(layer, 7)
                    gate_out(layer, 7, g)
                chunk(n0 + O0, hooks_o, split=split_y)
                with act.Fori(0, 7) as i:

                    def hooks_x(g):
                        f = layer * 8 + i + 8
                        if g == 4:
                            square_x(f, i)
                        if g in (9, 10):
                            copy_x(f, i, g - 9)
                    chunk(n0 + i + (O0 + 1), hooks_x)
                finish_x(layer * 8 + 15, 7)

        @block.vector
        def _(dve):
            def a_split_lo(s, g, scale):
                dve.wait_ge(a_hi, s * NG + (g + 1))
                for k in range(KG * g, KG * g + KG):
                    ins = dve.scalar_tensor_tensor(
                        out=alo[:, k, :], in0=F[:, k * SEQ:(k + 1) * SEQ], scalar=pc[:, scale + k:scale + k + 1],
                        in1=ahi[:, k, :].bitcast(F32), op0=ALU.mult, op1=ALU.subtract)
                ins.then_inc(a_lo, 1)

            def chunk(n, hooks=no_hooks, split=None):
                for g in range(NG):
                    dve.wait_ge(w_hi, n * NG + (g + 1))
                    dve.tensor_tensor(wlo[:, g % RING, :, :], raw[:, g % RING, :, :],
                                      whi[:, g % RING, :, :].bitcast(F32), ALU.subtract).then_inc(w_lo, 1)
                    hooks(g)
                    if split and g >= 1:
                        for k in ((0, 1) if g == 1 else (g,)):
                            split(k)

            def gla(layer, u, i, g):
                vcol = i * 2 * P
                if g == 4:
                    dve.wait_ge(G["e"], u * 2 + 1)
                    for t in range(T):
                        ins = dve.tensor_scalar(g_g[:, t * P:(t + 1) * P], M[0][:, t * P:(t + 1) * P], 0.0,
                                                rstd[:, t:t + 1], ALU.min, ALU.mult)
                    ins.then_inc(G["min"], 1)
                    dve.wait_ge(G["min"], u + 1)
                    dve.wait_ge(G["l1"], u + 1)
                    dve.tensor_tensor(g_g, g_g, g_l1, ALU.subtract).then_inc(G["g"], 1)
                if g == 6:
                    dve.wait_ge(G["exps"], u + 1)
                    dve.wait_ge(routed, layer * ROUTED + 5)
                    q = gq[:, :, ds(i * P, P)]
                    k = gk[:, :, ds(i * P, P)]
                    v3 = lambda a: a.rearrange("p (t n) -> p t n", t=T)
                    dve.scalar_tensor_tensor(out=v3(g_qd), in0=q, scalar=DK ** -0.5, in1=v3(g_eb),
                                             op0=ALU.mult, op1=ALU.mult)
                    dve.tensor_tensor(v3(g_kd), k, v3(g_enb), ALU.mult).then_inc(G["qkd"], 1)
                    for c in range(2):
                        r = slice(c * DK, (c + 1) * DK)
                        ins = dve.tensor_tensor(g_ks[r, :, c, :], gk[r, :, ds(i * P, P)],
                                                v3(g_es)[r, :, :], ALU.mult)
                    ins.then_inc(G["kst"], 1)
                if g == 10:
                    dve.wait_ge(G["U"], u + 1)
                    dve.wait_ge(G["dec"], u + 1)
                    for c, (bank, off) in enumerate(((4, 0), (4, 256), (5, 0))):
                        if c:
                            dve.wait_ge(G["S"], u * 3 + c)
                        for h in range(2):
                            r = slice(h * DK, (h + 1) * DK)
                            src = M[bank][r, off + h * P:off + (h + 1) * P]
                            if c == 0:
                                ins = dve.tensor_copy(g_S[r, 1, :], src)
                            else:
                                ins = dve.scalar_tensor_tensor(out=g_S[r, c + 1, :], in0=g_S[r, c, :],
                                                               scalar=g_dec[r, c:c + 1], in1=src,
                                                               op0=ALU.mult, op1=ALU.add)
                        ins.then_inc(G["S"], 1)
                if g == 11:
                    dve.wait_ge(G["AT"], u + 1)
                    dve.tensor_copy(g_AT, M[0][:, :]).then_inc(G["ATcopied"], 1)
                if g == 15:
                    dve.wait_ge(G["sq"], u + 1)
                    dve.tensor_reduce(g_rs[:, 0:4], g_sq.rearrange("p (k n) -> p k n", k=4), AX.X,
                                      ALU.add).then_inc(G["ssq"], 1)
                    dve.wait_ge(G["rstd"], u + 1)
                    for t in range(T):
                        for h in range(2):
                            b = (2 * t + h)
                            ins = dve.tensor_scalar(Y[:, t, ds(vcol + h * P, P)], M[1][:, b * P:(b + 1) * P],
                                                    g_rs[:, 4 + b:5 + b], None, ALU.mult)
                    ins.then_inc(G["y"], 1)

            def swa(u, i, g):
                if g == 0:
                    dve.tensor_copy(s_sm[:, 14:16].unsqueeze(2), pc[:, Q_SINK:Q_SINK + 16].rearrange(
                        "p (q h) -> p q h", q=2)[:, :, ds(i, 1)]).then_inc(S["par"], 1)
                    q = Y[:, :, ds(i * P + BW, P)]
                    sq = s_sq.rearrange("p (t n) -> p t n", t=T)
                    dve.tensor_tensor(sq, q, q, ALU.mult).then_inc(S["sq"], 1)
                    dve.wait_ge(S["sq"], u + 1)
                    dve.tensor_reduce(s_sm[:, 0:2], sq, AX.X, ALU.add).then_inc(S["ssq"], 1)
                if g == 1:
                    dve.wait_ge(S["rstd"], u + 1)
                    for t in range(T):
                        ins = dve.tensor_scalar(s_qn[:, t * P:(t + 1) * P], Y[:, t, ds(i * P + BW, P)],
                                                s_sm[:, 2 + t:3 + t], None, ALU.mult)
                    ins.then_inc(S["qn"], 1)
                if g == 9:
                    dve.wait_ge(S["scores"], u + 1)
                    dve.wait_ge(S["par"], u + 1)
                    dve.scalar_tensor_tensor(out=s_s, in0=dist_swa[:, :], scalar=s_sm[:, 15:16],
                                             in1=M[1][:, 0:384], op0=ALU.mult, op1=ALU.add).then_inc(S["s"], 1)
                    dve.wait_ge(S["s"], u + 1)
                    dve.tensor_reduce(s_sm[:, 4:5], s_s[:, 0:P], AX.X, ALU.max)
                    dve.tensor_reduce(s_sm[:, 5:6], s_s[:, P:3 * P], AX.X, ALU.max).then_inc(S["max"], 1)
                    dve.wait_ge(S["max"], u + 1)
                    dve.tensor_scalar(s_sm[:, 6:8], s_sm[:, 4:6], s_sm[:, 14:15], -1.0, ALU.max,
                                      ALU.mult).then_inc(S["neg"], 1)
                if g == 11:
                    dve.wait_ge(S["sink"], u + 1)
                    dve.tensor_tensor(s_sm[:, 12:14], s_sm[:, 8:10], s_sm[:, 10:12], ALU.add).then_inc(S["den"], 1)
                    dve.wait_ge(S["den"], u + 1)
                    dve.reciprocal(s_sm[:, 12:14], s_sm[:, 12:14]).then_inc(S["rden"], 1)
                if g == 12:
                    dve.wait_ge(S["pT"], u + 1)
                    dve.tensor_copy(s_pT, M[2][:, 0:384]).then_inc(S["pTc"], 1)
                if g == 15:
                    dve.wait_ge(S["o"], u + 1)
                    dve.wait_ge(S["rden"], u + 1)
                    for t in range(T):
                        ins = dve.tensor_scalar(Y[:, t, ds(i * P + BW, P)], M[3][:, t * P:(t + 1) * P],
                                                s_sm[:, 12 + t:13 + t], None, ALU.mult)
                    ins.then_inc(S["y"], 1)

            def lru(u, i, g):
                if g == 0:
                    dve.tensor_copy(l_par.unsqueeze(2), pc[:, Q_LRU:Q_LRU + 72].rearrange("p (q n) -> p q n", q=9)[:, :, ds(i, 1)]
                                    ).then_inc(L["par"], 1)
                if g == 7:
                    dve.wait_ge(L["turned"], u + 2)
                    dve.tensor_copy(l_x[:, 3:3 + SEQ], M[4][:, 0:256]).then_inc(L["x"], 1)
                    dve.wait_ge(L["x"], u + 1)
                    dve.wait_ge(L["par"], u + 1)
                    dve.tensor_scalar(l_xc, l_x[:, 3:3 + SEQ], l_par[:, 3:4], l_par[:, 4:5], ALU.mult,
                                      ALU.add).then_inc(L["c0"], 1)
                    for j, (prev, done) in enumerate((("c0", "c1"), ("c1", "c2"), ("c2", "xc"))):
                        dve.wait_ge(L[prev], u + 1)
                        dve.scalar_tensor_tensor(out=l_xc, in0=l_x[:, j:j + SEQ], scalar=l_par[:, j:j + 1],
                                                 in1=l_xc, op0=ALU.mult, op1=ALU.add).then_inc(L[done], 1)
                if g == 12:
                    dve.wait_ge(L["i"], u + 1)
                    dve.tensor_tensor(l_u, l_ri[:, 256:512], l_xc, ALU.mult).then_inc(L["ix"], 1)
                    dve.wait_ge(L["ln1"], u + 1)
                    dve.tensor_tensor(l_l2, l_l2, l_l1, ALU.subtract).then_inc(L["d"], 1)
                if g == 13:
                    dve.wait_ge(L["sf"], u + 1)
                    dve.wait_ge(L["ix"], u + 1)
                    dve.tensor_tensor(l_u, l_u, l_l2, ALU.mult).then_inc(L["u"], 1)
                    dve.wait_ge(L["u"], u + 1)
                    dve.wait_ge(L["a"], u + 1)
                    dve.tensor_tensor_scan(l_h, l_a, l_u, 0.0, ALU.mult, ALU.add).then_inc(L["h"], 1)
                if g == 15:
                    dve.wait_ge(L["hT"], u + 1)
                    dve.tensor_copy(Y[:, :, ds(i * P + 3 * BW, P)],
                                    M[4][:, 256:512].rearrange("p (t n) -> p t n", t=T)).then_inc(L["y"], 1)

            def diff(u, head, s):
                hcol = head * P
                v3 = lambda a: a.rearrange("p (t n) -> p t n", t=T)
                q, k = Y[:, :, ds(hcol + 2 * BW, P)], dk[:, :, ds(hcol, P)]
                if s == "sq":
                    dve.tensor_tensor(v3(d_sq[:, 0:256]), q, q, ALU.mult)
                    dve.tensor_tensor(v3(d_sq[:, 256:512]), k, k, ALU.mult).then_inc(DF["sqk"], 1)
                    dve.wait_ge(DF["sqk"], u + 1)
                    dve.tensor_reduce(d_sm[:, 0:8], d_sq.rearrange("p (k n) -> p k n", k=8), AX.X,
                                      ALU.add).then_inc(DF["ssq"], 1)
                if s == "norm":
                    dve.wait_ge(DF["rstd"], u + 1)
                    for src, dst, b in ((q, d_qn, 8), (k, d_kn, 12)):
                        for t in range(T):
                            ins = dve.tensor_tensor(
                                dst[:, t * P:(t + 1) * P].rearrange("p (c n) -> p c n", c=2),
                                src[:, t, :].rearrange("p (c n) -> p c n", c=2),
                                d_sm[:, b + 2 * t:b + 2 * t + 2].unsqueeze(2).to_broadcast([P, 2, DK]), ALU.mult)
                    ins.then_inc(DF["qkn"], 1)
                if s == "scores":
                    dve.tensor_copy(d_sm[:, 28:29], pc[:, ds(head + Q_SLOPE, 1)]).then_inc(DF["par"], 1)
                    dve.wait_ge(DF["scores"], u + 1)
                    dve.wait_ge(DF["par"], u + 1)
                    for c in range(2):
                        ins = dve.scalar_tensor_tensor(out=d_s[:, c * 384:(c + 1) * 384], in0=dist[:, :],
                                                       scalar=d_sm[:, 28:29], in1=M[1 + c][:, 0:384],
                                                       op0=ALU.mult, op1=ALU.add)
                    ins.then_inc(DF["s"], 1)
                    dve.wait_ge(DF["s"], u + 1)
                    s2 = d_s.rearrange("p (c n) -> p c n", c=2)
                    dve.tensor_reduce(d_sm[:, 16:18], s2[:, :, 0:P], AX.X, ALU.max)
                    dve.tensor_reduce(d_sm[:, 18:20], s2[:, :, P:384], AX.X, ALU.max).then_inc(DF["max"], 1)
                    dve.wait_ge(DF["max"], u + 1)
                    dve.tensor_scalar(d_sm[:, 20:24], d_sm[:, 16:20], -1.0, None, ALU.mult).then_inc(DF["neg"], 1)
                if s == "w":
                    dve.wait_ge(DF["p"], u + 1)
                    dve.reciprocal(d_sm[:, 24:28], d_sm[:, 24:28]).then_inc(DF["rp"], 1)
                    dve.wait_ge(DF["rp"], u + 1)
                    for t in range(T):
                        ins = dve.tensor_scalar(d_sm[:, 25 + 2 * t:26 + 2 * t], d_sm[:, 25 + 2 * t:26 + 2 * t],
                                                pc[:, Q_LAM:Q_LAM + 1], None, ALU.mult)
                    ins.then_inc(DF["coef"], 1)
                    dve.tensor_scalar(d_w[:, 0:P], d_p[:, 0:P], d_sm[:, 24:25], None, ALU.mult)
                    dve.tensor_scalar(d_w[:, P:384], d_p[:, P:384], d_sm[:, 26:27], None,
                                      ALU.mult).then_inc(DF["w0"], 1)
                    dve.wait_ge(DF["coef"], u + 1)
                    dve.wait_ge(DF["w0"], u + 1)
                    dve.scalar_tensor_tensor(out=d_w[:, 0:P], in0=d_p[:, 384:512], scalar=d_sm[:, 25:26],
                                             in1=d_w[:, 0:P], op0=ALU.mult, op1=ALU.add)
                    dve.scalar_tensor_tensor(out=d_w[:, P:384], in0=d_p[:, 512:768], scalar=d_sm[:, 27:28],
                                             in1=d_w[:, P:384], op0=ALU.mult, op1=ALU.add).then_inc(DF["w"], 1)
                if s == "wT":
                    dve.wait_ge(DF["wT"], u + 1)
                    dve.tensor_copy(d_wT, M[3][:, 0:384]).then_inc(DF["wTc"], 1)

            def gate_mult_y(layer, j):
                dve.wait_ge(main_free, (layer * CHUNKS + j + ROUTED + 2) * T)
                dve.tensor_tensor(stage[:, :, :], stage[:, :, :], Y[:, :, ds(j * NC, NC)],
                                  ALU.mult).then_inc(gate_mult, 1)

            def add_x(layer, i):
                f = layer * 8 + i + 8
                dve.wait_ge(x_loaded, (layer * 8 + i) * 16 + 16)
                dve.wait_ge(x_stored, f * 16)
                dve.wait_ge(x_F, f * 2 + 2)
                n = layer * CHUNKS + i + O0
                dve.wait_ge(main_ready, n + 1)
                dve.tensor_tensor(x_new[:, 0, :], x_old[:, 0, :], main[0][:, :], ALU.add).then_inc(main_free, 1)
                dve.wait_ge(w_used, n * NG + (NG + RING))
                dve.tensor_tensor(x_new[:, 1, :], x_old[:, 1, :], main[1][:, :], ALU.add).then_inc(main_free, 1)
                dve.wait_ge(main_free, (n + 2) * T)
                dve.sem_inc(x_added, 1)

            def x_rms(layer1):
                dve.wait_ge(x_squared, layer1 * 16 + 1)
                dve.tensor_reduce(small[:, 30:32], ssq[:, :, :], AX.X, ALU.add).then_inc(rs_sum, 1)


            dve.sem_inc(w_lo, RING)
            dve.sem_inc(a_lo, 1)
            dve.sem_inc(x_added, 9)
            dve.memset(one, 1.0).then_inc(par_math, 1)
            dve.memset(eps, EPS).then_inc(par_math, 1)
            dve.memset(tiny, 1e-19).then_inc(par_math, 1)
            for i in range(8):
                dve.wait_ge(x_in[i // 2], 16)
                for t in range(T):
                    if i + t:
                        dve.wait_ge(x_squared_in, i * T + t)
                    piece = Y[:, t, i * NC:(i + 1) * NC]
                    dve.tensor_tensor_reduce(cut(2560, NC), piece, piece, 1.0, 0.0, ALU.mult, ALU.add,
                                             ssq[:, t, i:i + 1]).then_inc(x_squared_in, 1)
            dve.wait_ge(x_squared_in, 8 * T)
            dve.sem_inc(x_squared, 8 * T)
            dve.wait_ge(setup_in, N_SETUP * 16)
            lq = cut(512, 512).rearrange("p (l q n) -> p l q n", l=2, q=4)
            for l in range(DEPTH):
                for s in range(2):
                    k = 2 * l + s
                    ins = dve.tensor_tensor_reduce(cut(1024 + k * DK, DK), lq[:, l, 2 * s, :],
                                                   lq[:, l, 2 * s + 1, :], 1.0, 0.0, ALU.mult, ALU.add,
                                                   small[:, k:k + 1])
            ins.then_inc(par_math, 1)
            dve.wait_ge(par_turned, 1)
            norm = par[:, :, Q_NORM:Q_NORM + KT]
            dve.tensor_copy(norm, M[0][:, 0:64].rearrange("p (l k) -> p l k", l=2)).then_inc(par_copied, 1)
            dve.tensor_copy(par[:, :, Q_LRU:Q_LRU + 32],
                            M[0][:, 64:128].rearrange("p (l k) -> p l k", l=2)).then_inc(par_copied, 1)
            m1 = M[1]
            for q in range(4):
                dve.tensor_copy(par[:, :, Q_LRU + 32 + 8 * q:Q_LRU + 40 + 8 * q],
                                m1[:, 16 * q:16 * q + 16].rearrange("p (l k) -> p l k", l=2)).then_inc(par_copied, 1)
            for col, off, scale in ((Q_SQ, 66, P ** -0.5), (Q_SK, 68, 1.0), (Q_DQ, 72, DK ** -0.5), (Q_DK, 74, 1.0)):
                for l in range(DEPTH):
                    dve.tensor_scalar(par[:, l, col:col + 1], m1[:, off + l:off + l + 1], scale, None,
                                      ALU.mult).then_inc(par_copied, 1)
            ys = par[:, :, Q_YS:Q_YS + KT]
            dve.memset(ys, 1.0).then_inc(par_math, 1)
            dve.wait_ge(par_math, 5)
            for l in range(DEPTH):
                lam_init = 0.8 - 0.6 * math.exp(-0.3 * l)
                dve.tensor_scalar(ys[:, l, 0:8], ys[:, l, 0:8], m1[:, 64 + l:65 + l], None,
                                  ALU.mult).then_inc(par_copied, 1)
                dve.tensor_scalar(ys[:, l, 16:24], ys[:, l, 16:24], m1[:, 70 + l:71 + l], 1.0 - lam_init,
                                  ALU.mult, ALU.mult).then_inc(par_copied, 1)
            dve.wait_ge(par_copied, 18)
            lam = cut(1584, 16)
            dve.tensor_copy(lam.rearrange("p (l n) -> p l n", l=2), par[:, :, Q_LRU + 56:Q_LRU + 64]
                            ).then_inc(par_copied, 1)
            dve.wait_ge(par_copied, 19)
            dve.tensor_scalar(cut(1600, 16), lam, -1.0, None, ALU.mult).then_inc(par_copied, 1)
            dve.wait_ge(par_copied, 20)
            dve.tensor_tensor(cut(1600, 16), cut(1600, 16), lam, ALU.max).then_inc(par_math, 1)
            dve.wait_ge(par_act, 2)
            chain = [20]

            def link(ins):
                chain[0] += 1
                ins.then_inc(par_copied, 1)
                dve.wait_ge(par_copied, chain[0])

            e, s, s2, a = cut(1600, 16), cut(1616, 16), cut(1632, 16), cut(1648, 16)
            link(dve.tensor_scalar(s2, e, 2.0, None, ALU.add))
            link(dve.reciprocal(s2, s2))
            link(dve.tensor_tensor(s, e, s2, ALU.mult))
            link(dve.tensor_tensor(s2, s, s, ALU.mult))
            link(dve.tensor_scalar(a, s2, 1.0 / 15, None, ALU.mult))
            for n in (13, 11, 9, 7, 5, 3):
                link(dve.scalar_tensor_tensor(out=a, in0=a, scalar=1.0 / n, in1=s2, op0=ALU.add, op1=ALU.mult))
            link(dve.scalar_tensor_tensor(out=a, in0=a, scalar=1.0, in1=s, op0=ALU.add, op1=ALU.mult))
            link(dve.tensor_scalar(a, a, 2.0, None, ALU.mult))
            link(dve.tensor_scalar(lam, lam, -1.0, 0.0, ALU.mult, ALU.max))
            link(dve.tensor_tensor(a, a, lam, ALU.add))
            a2 = a.rearrange("p (l n) -> p l n", l=2)
            link(dve.tensor_scalar(par[:, :, Q_LRU + 56:Q_LRU + 64], a2, 8.0, None, ALU.mult))
            link(dve.tensor_scalar(par[:, :, Q_LRU + 64:Q_LRU + 72], a2, -8.0, None, ALU.mult))
            for l in range(DEPTH):
                lam_init = 0.8 - 0.6 * math.exp(-0.3 * l)
                link(dve.tensor_scalar(small[:, 2 * l:2 * l + 1], small[:, 2 * l:2 * l + 1], lam_init, None, ALU.add))
                link(dve.tensor_tensor(par[:, l, Q_LAM:Q_LAM + 1], small[:, 2 * l + 1:2 * l + 2],
                                       small[:, 2 * l:2 * l + 1], ALU.subtract))
            dve.wait_ge(consts, 15 + HEADS)
            link(dve.tensor_scalar(dist_swa[:, :], dist[:, :], float(P), MASKED, ALU.is_ge, ALU.mult))
            link(dve.tensor_tensor(dist_swa[:, :], dist_swa[:, :], dist[:, :], ALU.max))

            with dve.Fori(0, DEPTH) as layer:
                n0 = layer * CHUNKS
                dve.wait_ge(a_lo, layer * 2 * NG + 1)
                dve.tensor_copy(pc[:, :], par[:, ds(layer, 1), :].rearrange("p a n -> p (a n)")
                                ).then_inc(now_ready, 1)

                def split_x(g):
                    if g == 0:
                        dve.wait_ge(now_ready, layer + 1)
                        dve.wait_ge(w_used, n0 * NG + RING)
                    a_split_lo(layer * 2, g, Q_NORM)

                def hooks_first(g):
                    if g == 4:
                        x_rms(layer + 1)
                        dve.memset(inv_rms[:, :, :], 0.0).then_inc(inv_zero, 1)
                    if g == 8:
                        dve.wait_ge(wa_hi_s, layer + 1)
                        dve.tensor_tensor(wa_lo[:, :, :], wa_raw, wa_hi[:, :, :].bitcast(F32),
                                          ALU.subtract).then_inc(wa_lo_s, 1)
                    if g == 10:
                        dve.wait_ge(rs_ready, layer + 1)
                        dve.wait_ge(inv_zero, layer + 1)
                        dve.reciprocal(inv_rms[:, :, RANK:RANK + 1], rstd[:, :].unsqueeze(2)).then_inc(inv_ready, 1)
                chunk(n0, hooks_first, split=split_x)
                with dve.Fori(0, 3) as i:
                    chunk(n0 + i + 1)
                dve.memset(g_ks, 0.0)
                dve.memset(g_q0, 0.0)
                dve.memset(g_q1, 0.0)
                dve.memset(g_S[:, 0, :], 0.0).then_inc(gla_zero, 1)
                with dve.Fori(0, 4) as i:
                    chunk(n0 + i + B0, lambda g: gla(layer, layer * 4 + i, i, g))
                dve.wait_ge(routed, layer * ROUTED + 8)
                for t in range(T):
                    for h in range(2):
                        b = 2 * h + t
                        k = skv[:, t, h * P:(h + 1) * P]
                        ins = dve.tensor_tensor_reduce(cut(b * P, P), k, k, 1.0, 0.0, ALU.mult, ALU.add,
                                                       s_sm[:, b:b + 1])
                ins.then_inc(K["ssq"], 1)
                dve.wait_ge(K["rstd"], layer + 1)
                for t in range(T):
                    for h in range(2):
                        b = 2 * h + t
                        ins = dve.tensor_scalar(cut(b * P, P), skv[:, t, h * P:(h + 1) * P],
                                                s_sm[:, 4 + b:5 + b], None, ALU.mult)
                ins.then_inc(K["kn"], 1)
                dve.memset(l_x[:, 0:3], 0.0).then_inc(lru_zero, 1)
                with dve.Fori(0, 8) as i:
                    u = layer * 8 + i

                    def hooks_c(g):
                        swa(u, i, g)
                        lru(u, i, g)
                    chunk(n0 + i + C0, hooks_c)
                dve.wait_ge(routed, layer * ROUTED + 16)
                dve.memset(d_q[0], 0.0)
                dve.memset(d_q[1], 0.0).then_inc(diff_zero, 1)
                diff(layer * 8, 0, "sq")
                diff(layer * 8, 0, "norm")
                def hooks_d(i, g, last=False):
                    if g == 2:
                        gate_mult_y(layer, i)
                    for h in range(2):
                        diff(layer * 8 + i * 2 + h, i * 2 + h, DIFF_DVE[h].get(g))
                    if g in (3, 5, 13, 15) and not (last and g > 5):
                        h = 1 if g <= 5 else 2
                        diff(layer * 8 + i * 2 + h, i * 2 + h, {3: "sq", 5: "norm", 13: "sq", 15: "norm"}[g])

                with dve.Fori(0, 3) as i:
                    chunk(n0 + i + D0, lambda g: hooks_d(i, g))
                chunk(n0 + D0 + 3, lambda g: hooks_d(3, g, last=True))
                with dve.Fori(0, 3) as i:
                    chunk(n0 + i + E0, lambda g: gate_mult_y(layer, i + 4) if g == 2 else None)
                chunk(n0 + O0, lambda g: gate_mult_y(layer, 7) if g == 2 else None,
                      split=lambda g: a_split_lo(layer * 2 + 1, g, Q_YS))
                with dve.Fori(0, 7) as i:
                    chunk(n0 + i + (O0 + 1), lambda g: add_x(layer, i) if g == 1 else None)
                add_x(layer, 7)

        @block.tensor
        def _(pe):
            def mm(out_, lhsT, rhs, start, stop):
                return pe.matmul(out_, lhsT, rhs, start=start, stop=stop, skip_group_check=True)

            def chunk(n, s, hooks=no_hooks):
                for g in range(NG):
                    pe.wait_ge(w_lo, n * NG + (g + 1 + RING))
                    pe.wait_ge(a_lo, s * NG + (g + 2))
                    slot = g % RING
                    for t in range(T):
                        if g == 0:
                            pe.wait_ge(main_free, n * T + (t + 1))
                        tt = slice(t * P, (t + 1) * P)
                        for k in range(KG):
                            kt = KG * g + k
                            mm(main[t][:, :], ahi[:, kt, tt], whi[:, slot, k, :], kt == 0, False)
                            mm(main[t][:, :], ahi[:, kt, tt], wlo[:, slot, k, :], False, False)
                            ins = mm(main[t][:, :], alo[:, kt, tt], whi[:, slot, k, :], False, kt == KT - 1)
                        if g == NG - 1 and t == 0:
                            ins.then_inc(main_ready, 1)
                    ins.then_inc(w_used, 1)
                    hooks(g)

            def turn_x(f, halves=(0, 1)):
                for half in halves:
                    pe.wait_ge(x_F, f * 2 + (half + 1))
                    for k in range(2):
                        for t in range(T):
                            if half == 0 and k == 0 and t == 0:
                                pe.wait_ge(x_added, f + 2)
                            c = 2 * half + k
                            ins = pe.transpose(M[half][:, (2 * k + t) * P:(2 * k + t + 1) * P],
                                               x_new[:, t, c * P:(c + 1) * P], ident[:, :])
                    ins.then_inc(x_T, 1)

            def gla(u, i, g):
                vcol = i * 2 * P
                if g == 1:
                    for t in range(T):
                        ins = mm(M[0][:, t * P:(t + 1) * P], g_aT[:, t * P:(t + 1) * P],
                                 g_wup[:, ds(i * P, P)], t == 0, True)
                    ins.then_inc(G["logit"], 1)
                if g == 3:
                    pe.wait_ge(G["g"], u + 1)
                    pe.wait_ge(G["y"], u + 1)
                    for t in range(T):
                        mm(M[1][:, t * P:(t + 1) * P], tri[:, :], g_g[:, t * P:(t + 1) * P], t == 0, True)
                        mm(M[1][:, 256 + t * P:256 + (t + 1) * P], suf[:, :], g_g[:, t * P:(t + 1) * P], False, True)
                        ins = mm(M[2][:, 2 * t:2 * t + 2], g_g[:, t * P:(t + 1) * P], chunk1[:, :], t == 0, True)
                    ins.then_inc(G["sums"], 1)
                if g == 6:
                    pe.wait_ge(G["qkd"], u + 1)
                    for t in range(T):
                        pe.transpose(M[3][:, t * P:(t + 1) * P], g_qd[:, t * P:(t + 1) * P], ident[:, :])
                        ins = pe.transpose(M[3][:, 256 + t * P:256 + (t + 1) * P], g_kd[:, t * P:(t + 1) * P],
                                           ident[:, :])
                    ins.then_inc(G["turned"], 1)
                    pe.wait_ge(G["kst"], u + 1)
                    for bank, off, t, c in ((4, 0, 0, 0), (4, 256, 0, 1), (5, 0, 1, 0)):
                        ins = mm(M[bank][:, off:off + 256], g_ks[:, t, c, :], Y[:, t, ds(vcol, 2 * P)], off == 0, True)
                    ins.then_inc(G["U"], 1)
                if g == 8:
                    pe.wait_ge(G["qkT"], u + 1)
                    for t in range(T):
                        for h in range(2):
                            b = 2 * t + h
                            ins = mm(M[0][:, b * P:(b + 1) * P], g_kT[:, t * P:(t + 1) * P],
                                     (g_q0, g_q1)[h][:, t * P:(t + 1) * P], b == 0, True)
                    ins.then_inc(G["AT"], 1)
                if g == 11:
                    pe.wait_ge(G["S"], u * 3 + 3)
                    for c in range(2):
                        r = slice(c * DK, (c + 1) * DK)
                        for t in range(T):
                            for h in range(2):
                                b = 2 * t + h
                                mm(M[1][r, b * P:(b + 1) * P], (g_q0, g_q1)[h][:, t * P + c * DK:t * P + (c + 1) * DK],
                                   g_S[:, 2 * t + c, :], b == 0, False)
                    pe.wait_ge(G["ATmasked"], u * 2 + 2)
                    for t in range(T):
                        for h in range(2):
                            b = 2 * t + h
                            ins = mm(M[1][:, b * P:(b + 1) * P], g_AT[:, b * P:(b + 1) * P],
                                     Y[:, t, ds(vcol + h * P, P)], False, True)
                    ins.then_inc(G["o"], 1)

            def swa(layer, u, i, g):
                kv = (i // 4) * 256
                if g == 3:
                    pe.wait_ge(K["kT"], layer + 1)
                    pe.wait_ge(S["qn"], u + 1)
                    for t in range(T):
                        ins = pe.transpose(M[0][:, t * P:(t + 1) * P], s_qn[:, t * P:(t + 1) * P], ident[:, :])
                    ins.then_inc(S["turned"], 1)
                if g == 5:
                    pe.wait_ge(S["qT"], u + 1)
                    mm(M[1][:, 0:P], s_qT[:, 0:P], kT_swa[:, ds(kv, P)], True, True)
                    mm(M[1][:, P:3 * P], s_qT[:, P:2 * P], kT_swa[:, ds(kv, 2 * P)], False, True).then_inc(S["scores"], 1)
                if g == 8:
                    pe.wait_ge(S["p"], u + 1)
                    for b in range(3):
                        ins = pe.transpose(M[2][:, b * P:(b + 1) * P], s_p[:, b * P:(b + 1) * P], ident[:, :])
                    ins.then_inc(S["pT"], 1)
                if g == 11:
                    pe.wait_ge(S["pTc"], u + 1)
                    pe.wait_ge(S["y"], u + 1)
                    vc = (i // 4) * P + 2 * P
                    mm(M[3][:, 0:P], s_pT[:, 0:P], skv[:, 0, ds(vc, P)], True, True)
                    mm(M[3][:, P:2 * P], s_pT[:, P:2 * P], skv[:, 0, ds(vc, P)], False, False)
                    mm(M[3][:, P:2 * P], s_pT[:, 2 * P:3 * P], skv[:, 1, ds(vc, P)], False, True).then_inc(S["o"], 1)

            def lru(layer, u, i, g):
                if g == 3:
                    pe.wait_ge(L["rx"], u + 1)
                    for t in range(T):
                        ins = pe.transpose(M[4][:, t * P:(t + 1) * P], l_rx[:, t * P:(t + 1) * P], ident[:, :])
                    ins.then_inc(L["turned"], 1)
                if g == 6:
                    pe.wait_ge(L["xc"], u + 1)
                    pe.wait_ge(L["w_landed"], u * 32 + 32)
                    mm(M[5][:, 0:256], l_w[:, 0, :], l_xc, True, True)
                    mm(M[5][:, 256:512], l_w[:, 1, :], l_xc, False, True).then_inc(L["gates"], 1)
                if g == 12:
                    pe.wait_ge(L["h"], u + 1)
                    for t in range(T):
                        ins = pe.transpose(M[4][:, 256 + t * P:256 + (t + 1) * P], l_h[:, t * P:(t + 1) * P],
                                           ident[:, :])
                    ins.then_inc(L["hT"], 1)

            def diff(u, hcol, s):
                if s == "turn":
                    pe.wait_ge(DF["qkn"], u + 1)
                    for t in range(T):
                        pe.transpose(M[0][:, t * P:(t + 1) * P], d_qn[:, t * P:(t + 1) * P], ident[:, :])
                        ins = pe.transpose(M[0][:, 256 + t * P:256 + (t + 1) * P], d_kn[:, t * P:(t + 1) * P],
                                           ident[:, :])
                    ins.then_inc(DF["turned"], 1)
                if s == "scores":
                    pe.wait_ge(DF["qkT"], u + 1)
                    for c in range(2):
                        mm(M[1 + c][:, 0:P], d_q[c][:, 0:P], d_kT[:, 0:P], True, True)
                        ins = mm(M[1 + c][:, P:3 * P], d_q[c][:, P:2 * P], d_kT, False, True)
                    ins.then_inc(DF["scores"], 1)
                if s == "wT":
                    pe.wait_ge(DF["w"], u + 1)
                    for b in range(3):
                        ins = pe.transpose(M[3][:, b * P:(b + 1) * P], d_w[:, b * P:(b + 1) * P], ident[:, :])
                    ins.then_inc(DF["wT"], 1)
                if s == "o":
                    pe.wait_ge(DF["wTc"], u + 1)
                    pe.wait_ge(DF["y"], u + 1)
                    mm(M[4][:, 0:P], d_wT[:, 0:P], dv[:, 0, ds(hcol, P)], True, True)
                    mm(M[4][:, P:2 * P], d_wT[:, P:2 * P], dv[:, 0, ds(hcol, P)], False, False)
                    mm(M[4][:, P:2 * P], d_wT[:, 2 * P:3 * P], dv[:, 1, ds(hcol, P)], False, True).then_inc(DF["o"], 1)

            def turn_gated(layer, j, g, hooks=(4, 7)):
                if g in hooks:
                    half = hooks.index(g)
                    pe.wait_ge(gate_mult, layer * 8 + (j + 1))
                    pe.wait_ge(gate_F, layer * 16 + (j * 2 + half + 1))
                    for k in range(2):
                        for t in range(T):
                            c = 2 * half + k
                            ins = pe.transpose(M[5][:, (2 * k + t) * P:(2 * k + t + 1) * P],
                                               stage[:, t, c * P:(c + 1) * P], ident[:, :])
                    ins.then_inc(gate_T, 1)

            pe.sem_inc(w_used, RING)
            pe.sem_inc(L["gates"], 1)
            pe.sem_inc(L["turned"], 1)
            pe.sem_inc(G["y"], 1)
            pe.sem_inc(S["y"], 1)
            pe.sem_inc(x_F, 2)
            def turn_input(q):
                pe.wait_ge(x_in[q // 4], 16)
                if q >= 4:
                    pe.wait_ge(x_F, q - 1)
                for k in range(2):
                    for t in range(T):
                        c = 2 * q + k
                        ins = pe.transpose(M[2 + q % 4][:, (2 * k + t) * P:(2 * k + t + 1) * P],
                                           Y[:, t, c * P:(c + 1) * P], ident[:, :])
                ins.then_inc(x_T, 1)

            pe.wait_ge(consts, 15 + HEADS)
            for q in range(NG // 2):
                turn_input(q)
            pe.wait_ge(setup_in, N_SETUP * 16)
            pe.transpose(M[0][:, 0:P], MIX[:, 0:P], ident[:, :])
            pe.transpose(M[1][:, 0:76], MIX[0:76, P:2 * P], ident[0:76, 0:76]).then_inc(par_turned, 1)
            for q in range(NG // 2, NG):
                turn_input(q)
            pe.wait_ge(par_copied, 18)
            with pe.Fori(0, DEPTH) as layer:
                n0 = layer * CHUNKS
                sx, sy = layer * 2, layer * 2 + 1
                chunk(n0, sx)
                pe.wait_ge(inv_ready, layer + 1)
                pe.wait_ge(x_F, layer * 16 + 18)
                for t in range(T):
                    mm(M[1][0:RANK + 1, t * P:(t + 1) * P], inv_rms[:, t, :], ident[:, :], t == 0, True)
                pe.wait_ge(wa_lo_s, layer + 1)
                for k in range(KT):
                    o = M[1][0:RANK, 0:SEQ]
                    mm(o, wa_hi[:, k, :], ahi[:, k, :], False, False)
                    mm(o, wa_lo[:, k, :], ahi[:, k, :], False, False)
                    ins = mm(o, wa_hi[:, k, :], alo[:, k, :], False, k == KT - 1)
                ins.then_inc(a_sum, 1)
                with pe.Fori(0, 3) as i:
                    chunk(n0 + i + 1, sx)
                pe.wait_ge(a_ready, layer + 1)
                pe.wait_ge(gla_zero, layer + 1)
                pe.wait_ge(a_up, layer * 32 + 32)
                pe.sem_inc(pe_passed, 1)
                with pe.Fori(0, 4) as i:
                    chunk(n0 + i + B0, sx, lambda g: gla(layer * 4 + i, i, g))
                pe.wait_ge(K["kn"], layer + 1)
                for b in range(4):
                    ins = pe.transpose(M[0][:, b * P:(b + 1) * P], cut(b * P, P), ident[:, :])
                ins.then_inc(K["turned"], 1)
                with pe.Fori(0, 8) as i:
                    u = layer * 8 + i

                    def hooks_c(g):
                        swa(layer, u, i, g)
                        lru(layer, u, i, g)
                    chunk(n0 + i + C0, sx, hooks_c)
                with pe.Fori(0, 4) as i:

                    def hooks_d(g):
                        for h in range(2):
                            diff(layer * 8 + i * 2 + h, i * 2 * P + h * P, DIFF_PE[h].get(g))
                        turn_gated(layer, i, g)
                    chunk(n0 + i + D0, sx, hooks_d)
                with pe.Fori(0, 3) as i:
                    chunk(n0 + i + E0, sx, lambda g: turn_gated(layer, i + 4, g))
                chunk(n0 + O0, sy, lambda g: turn_gated(layer, 7, g))
                with pe.Fori(0, 7) as i:
                    chunk(n0 + i + (O0 + 1), sy, lambda g: turn_x(layer * 8 + i + 8, (g - 5,)) if g in (5, 6) else None)
                turn_x(layer * 8 + 15)


_INS = ['x', 'norm_w', 'w_in', 'w_out', 'gla_w_up', 'gla_b_up', 'gla_norm_w', 'swa_q_norm', 'swa_k_norm',
        'swa_sinks', 'diff_q_norm', 'diff_k_norm', 'diff_lq1', 'diff_lk1', 'diff_lq2', 'diff_lk2',
        'diff_out_norm', 'lru_conv_w', 'lru_conv_b', 'lru_w_r', 'lru_b_r', 'lru_w_i', 'lru_b_i', 'lru_lambda']


def kernel(**inputs):
    import numpy as _np
    import concourse.bacc as _bacc
    from concourse import mybir as _mybir
    from concourse.bass_utils import run_bass_kernel_spmd as _run

    nc = _bacc.Bacc("TRN2", target_bir_lowering=False, num_devices=1)
    arrays, args = {}, []
    for name in _INS:
        a = _np.ascontiguousarray(inputs[name])
        arrays[f"in_{name}"] = a
        args.append(nc.dram_tensor(f"in_{name}", a.shape, _mybir.dt.from_np(a.dtype), kind="ExternalInput").ap())
    shape = inputs['x'].shape
    args.append(nc.dram_tensor("out", shape, _mybir.dt.from_np(_np.dtype('float32')), kind="ExternalOutput").ap())
    hybrid_trunk(nc, *args)
    r = _run(nc, [arrays], core_ids=[0])
    return r.results[0]["out"]
```
